# Optimizing a Trainium2 kernel written in Bass

```python
import math
import jax, jax.numpy as jnp
from jax import lax
import numpy as np

D_MODEL = 1024
BATCH = 1
SEQ = 1024
DEPTH = 1
DEC_BATCH = 1
DEC_SEQ = 64
PAST_LEN = 512

CHUNK = 64
D_MIX = D_MODEL
RW_WIDTH = D_MIX // 2
RW_HD = 64
RW_HEADS = RW_WIDTH // RW_HD
RW_W_RANK = 64
RW_A_RANK = 64
RW_G_RANK = 128
RW_COLS = 3 * RW_WIDTH + RW_W_RANK + RW_A_RANK + RW_G_RANK
RW_GN_EPS = 64e-5
DA_WIDTH = D_MIX - RW_WIDTH
DA_HEADS = 4
DA_HD = 64
DA_VD = 2 * DA_HD
DA_COLS = 3 * DA_WIDTH
DA_SCALE = 1.0 / math.sqrt(DA_HD)
ROT_DIM = DA_HD // 4
ROPE_THETA = 500000.0
Q_BLOCK = 128
IN_COLS = RW_COLS + DA_COLS
PEER_HEADS = 8
PEER_NKEYS = 128
PEER_N = PEER_NKEYS * PEER_NKEYS
PEER_DK = 256
PEER_HALF = PEER_DK // 2
PEER_TOPK = 16
PEER_BLOCK = 128
LN_EPS = 1e-5
ALPHA = (2.0 * DEPTH) ** 0.25
BETA = (8.0 * DEPTH) ** -0.25

kernel_name = 'hymba_rwkv7_diffattn_peer_stream_step'

def _layer_norm(x, g, b):
    xf = x.astype(jnp.float32)
    mu = jnp.mean(xf, -1, keepdims=True)
    xc = xf - mu
    var = jnp.mean(xc * xc, -1, keepdims=True)
    y = xc * lax.rsqrt(var + LN_EPS) * g.astype(jnp.float32) + b.astype(jnp.float32)
    return y.astype(x.dtype)

def _rope_partial(x, pos):
    half = ROT_DIM // 2
    inv = jnp.power(ROPE_THETA, -jnp.arange(half, dtype=jnp.float32) * (2.0 / ROT_DIM))
    ang = pos.astype(jnp.float32)[:, None] * inv[None, :]
    cos = jnp.cos(ang)[None, :, None, None, :]
    sin = jnp.sin(ang)[None, :, None, None, :]
    xr = x[..., :ROT_DIM].astype(jnp.float32)
    x1, x2 = xr[..., :half], xr[..., half:]
    rot = jnp.concatenate([x1 * cos - x2 * sin, x2 * cos + x1 * sin], -1).astype(x.dtype)
    return jnp.concatenate([rot, x[..., ROT_DIM:]], -1)

def _wkv_scan(r, w, k, v, kk, b, s0):
    def step(S, inp):
        r_t, w_t, k_t, v_t, kk_t, b_t = inp
        sa = jnp.einsum('bhvk,bhk->bhv', S, kk_t)
        S = S * w_t[:, :, None, :] - sa[..., None] * b_t[:, :, None, :] + v_t[..., None] * k_t[:, :, None, :]
        y = jnp.einsum('bhvk,bhk->bhv', S, r_t)
        return S, y
    xs = tuple(jnp.moveaxis(t, 1, 0) for t in (r, w, k, v, kk, b))
    s_fin, ys = lax.scan(step, s0, xs)
    return jnp.moveaxis(ys, 0, 1), s_fin

def _rwkv7_group(p, shift_prev, s0, mu, w0, w2, a0, a2, g2, k_k, k_a, r_k, lnx_g, lnx_b):
    B, T, _ = p.shape
    f32 = jnp.float32
    pf = p.astype(f32)
    prev = jnp.concatenate([shift_prev.astype(f32), pf[:, :-1]], axis=1)
    pm = pf + (prev - pf) * mu.astype(f32)
    W = RW_WIDTH
    o1 = 3 * W
    o2 = o1 + RW_W_RANK
    o3 = o2 + RW_A_RANK
    r, k, v = pm[..., :W], pm[..., W:2 * W], pm[..., 2 * W:o1]
    wl, al, gl = pm[..., o1:o2], pm[..., o2:o3], pm[..., o3:]
    w = -jax.nn.softplus(-(w0.astype(f32) + jnp.tanh(wl) @ w2.astype(f32))) - 0.5
    decay = jnp.exp(-jnp.exp(w))
    a = jax.nn.sigmoid(a0.astype(f32) + al @ a2.astype(f32))
    g = jax.nn.sigmoid(gl) @ g2.astype(f32)
    heads = lambda t: t.reshape(B, T, RW_HEADS, RW_HD)
    kk = heads(k * k_k.astype(f32))
    kk = kk / jnp.maximum(jnp.sqrt(jnp.sum(kk * kk, -1, keepdims=True)), 1e-12)
    k = k * (1.0 + (a - 1.0) * k_a.astype(f32))
    rh, kh, vh, ah, dh = heads(r), heads(k), heads(v), heads(a), heads(decay)
    y, s_fin = _wkv_scan(rh, dh, kh, vh, kk, kk * ah, s0.astype(f32))
    ym = jnp.mean(y, -1, keepdims=True)
    yc = y - ym
    yv = jnp.mean(yc * yc, -1, keepdims=True)
    yn = (yc * lax.rsqrt(yv + RW_GN_EPS)).reshape(B, T, W) * lnx_g.astype(f32) + lnx_b.astype(f32)
    bonus = (jnp.sum(rh * kh * r_k.astype(f32), -1, keepdims=True) * vh).reshape(B, T, W)
    out = (yn + bonus) * g
    return out.astype(p.dtype), p[:, -1:], s_fin.astype(s0.dtype)

def _diff_maps(qb, k, v, lam, mask):
    s = jnp.einsum('bqhcd,bkhcd->bhcqk', qb.astype(jnp.float32), k.astype(jnp.float32)) * DA_SCALE
    if mask is not None:
        s = jnp.where(mask, s, -jnp.inf)
    pm = jax.nn.softmax(s, axis=-1)
    att = pm[:, :, 0] - lam * pm[:, :, 1]
    return jnp.einsum('bhqk,bkhe->bqhe', att, v.astype(jnp.float32))

def _diff_attn_prompt(q, k, v, lam):
    B, T = q.shape[0], q.shape[1]
    nb = T // Q_BLOCK
    kchunk = jnp.arange(T) // CHUNK
    def blk(i):
        start = i * Q_BLOCK
        qb = lax.dynamic_slice_in_dim(q, start, Q_BLOCK, axis=1)
        qchunk = (start + jnp.arange(Q_BLOCK)) // CHUNK
        mask = (kchunk[None, :] <= qchunk[:, None])[None, None, None]
        return _diff_maps(qb, k, v, lam, mask)
    o = lax.map(blk, jnp.arange(nb))
    return jnp.moveaxis(o, 0, 1).reshape(B, T, DA_HEADS, DA_VD)

def _mixer(h, pos, shift_prev, s0, ck, cv, w_in, shift_mu, rw_w0, rw_w2, rw_a0, rw_a2, rw_g2,
           rw_kk, rw_ka, rw_rk, rw_lnx_g, rw_lnx_b, da_lq1, da_lk1, da_lq2, da_lk2, da_subln_g,
           w_out, lam_init):
    B, T, _ = h.shape
    proj = h @ w_in
    p_rw, p_da = proj[..., :RW_COLS], proj[..., RW_COLS:]
    rw_out, new_shift, new_s = _rwkv7_group(p_rw, shift_prev, s0, shift_mu, rw_w0, rw_w2, rw_a0,
                                            rw_a2, rw_g2, rw_kk, rw_ka, rw_rk, rw_lnx_g, rw_lnx_b)
    q = p_da[..., :DA_WIDTH].reshape(B, T, DA_HEADS, 2, DA_HD)
    k = p_da[..., DA_WIDTH:2 * DA_WIDTH].reshape(B, T, DA_HEADS, 2, DA_HD)
    v = p_da[..., 2 * DA_WIDTH:].reshape(B, T, DA_HEADS, DA_VD)
    q = _rope_partial(q, pos)
    k = _rope_partial(k, pos)
    f32 = jnp.float32
    lam = (jnp.exp(jnp.sum(da_lq1.astype(f32) * da_lk1.astype(f32)))
           - jnp.exp(jnp.sum(da_lq2.astype(f32) * da_lk2.astype(f32))) + lam_init)
    if ck is None:
        o = _diff_attn_prompt(q, k, v, lam)
    else:
        P = ck.shape[1]
        k_all = jnp.concatenate([ck.reshape(B, P, DA_HEADS, 2, DA_HD).astype(k.dtype), k], axis=1)
        v_all = jnp.concatenate([cv.astype(v.dtype), v], axis=1)
        o = _diff_maps(q, k_all, v_all, lam, None)
    o = o * lax.rsqrt(jnp.mean(o * o, -1, keepdims=True) + LN_EPS) * da_subln_g.astype(f32) * (1.0 - lam_init)
    da_out = o.reshape(B, T, DA_WIDTH).astype(h.dtype)
    m = jnp.concatenate([rw_out, da_out], axis=-1) @ w_out
    return m, k.reshape(B, T, DA_HEADS, 2 * DA_HD), v, new_s, new_shift

def _peer(h, wq, subkeys, u_tab, v_tab):
    B, T, D = h.shape
    n = B * T
    nb = -(-n // PEER_BLOCK)
    xf = jnp.pad(h.reshape(n, D), ((0, nb * PEER_BLOCK - n), (0, 0))).reshape(nb, PEER_BLOCK, D)
    f32 = jnp.float32
    def blk(xb):
        q = (xb @ wq).reshape(PEER_BLOCK, PEER_HEADS, 2, PEER_HALF).astype(f32)
        s = jnp.einsum('thcd,hcnd->thcn', q, subkeys.astype(f32))
        s1, i1 = lax.top_k(s[:, :, 0], PEER_TOPK)
        s2, i2 = lax.top_k(s[:, :, 1], PEER_TOPK)
        cand = (s1[..., :, None] + s2[..., None, :]).reshape(PEER_BLOCK, PEER_HEADS, PEER_TOPK * PEER_TOPK)
        cidx = (i1[..., :, None] * PEER_NKEYS + i2[..., None, :]).reshape(PEER_BLOCK, PEER_HEADS, PEER_TOPK * PEER_TOPK)
        top, sel = lax.top_k(cand, PEER_TOPK)
        idx = jnp.take_along_axis(cidx, sel, axis=-1)
        gate = jax.nn.softmax(top, axis=-1)
        u = jnp.take(u_tab, idx, axis=0).astype(f32)
        act = jax.nn.gelu(jnp.einsum('thed,td->the', u, xb.astype(f32)), approximate=False)
        vv = jnp.take(v_tab, idx, axis=0).astype(f32)
        return jnp.einsum('the,thed->td', gate * act, vv).astype(xb.dtype)
    out = lax.map(blk, xf).reshape(nb * PEER_BLOCK, D)[:n]
    return out.reshape(B, T, D)

def setup_inputs(seed: int = 0) -> dict:
    key = jax.random.key(seed)
    ks = jax.random.split(key, 40)
    nrm = lambda i, shape, s: s * jax.random.normal(ks[i], shape, jnp.float32)
    L = DEPTH
    vscale = jnp.concatenate([
        jnp.ones((2 * RW_WIDTH,), jnp.float32), jnp.full((RW_WIDTH,), BETA, jnp.float32),
        jnp.ones((RW_W_RANK + RW_A_RANK + RW_G_RANK + 2 * DA_WIDTH,), jnp.float32),
        jnp.full((DA_WIDTH,), BETA, jnp.float32)])
    return {
        'x_prompt': nrm(0, (BATCH, SEQ, D_MODEL), 1.0),
        'x_sample': nrm(1, (DEC_BATCH, DEC_SEQ, D_MODEL), 1.0),
        'cache_k': nrm(2, (L, DEC_BATCH, PAST_LEN, DA_HEADS, 2 * DA_HD), 1.0),
        'cache_v': nrm(3, (L, DEC_BATCH, PAST_LEN, DA_HEADS, DA_VD), 1.0),
        'state_wkv': nrm(4, (L, DEC_BATCH, RW_HEADS, RW_HD, RW_HD), 0.1),
        'state_shift': nrm(5, (L, DEC_BATCH, 1, RW_COLS), 1.0),
        'ln_in_g': 1.0 + nrm(6, (D_MODEL,), 0.02),
        'ln_in_b': nrm(7, (D_MODEL,), 0.02),
        'w_in': nrm(8, (L, D_MODEL, IN_COLS), D_MODEL ** -0.5) * vscale,
        'shift_mu': jax.random.uniform(ks[9], (L, RW_COLS), jnp.float32),
        'rw_w0': jax.random.uniform(ks[10], (L, RW_WIDTH), jnp.float32, -5.0, 1.0),
        'rw_w2': nrm(11, (L, RW_W_RANK, RW_WIDTH), 0.1),
        'rw_a0': nrm(12, (L, RW_WIDTH), 0.1),
        'rw_a2': nrm(13, (L, RW_A_RANK, RW_WIDTH), RW_A_RANK ** -0.5),
        'rw_g2': nrm(14, (L, RW_G_RANK, RW_WIDTH), RW_G_RANK ** -0.5),
        'rw_kk': 0.85 + nrm(15, (L, RW_WIDTH), 0.05),
        'rw_ka': 1.0 + nrm(16, (L, RW_WIDTH), 0.05),
        'rw_rk': nrm(17, (L, RW_HEADS, RW_HD), 0.1),
        'rw_lnx_g': 1.0 + nrm(18, (L, RW_WIDTH), 0.02),
        'rw_lnx_b': nrm(19, (L, RW_WIDTH), 0.02),
        'da_lq1': nrm(20, (L, DA_HD), 0.1),
        'da_lk1': nrm(21, (L, DA_HD), 0.1),
        'da_lq2': nrm(22, (L, DA_HD), 0.1),
        'da_lk2': nrm(23, (L, DA_HD), 0.1),
        'da_subln_g': 1.0 + nrm(24, (L, DA_VD), 0.02),
        'w_out': nrm(25, (L, D_MIX, D_MODEL), BETA * D_MIX ** -0.5),
        'ln1_g': 1.0 + nrm(26, (L, D_MODEL), 0.02),
        'ln1_b': nrm(27, (L, D_MODEL), 0.02),
        'peer_wq': nrm(28, (L, D_MODEL, PEER_HEADS * PEER_DK), D_MODEL ** -0.5),
        'peer_subkeys': nrm(29, (L, PEER_HEADS, 2, PEER_NKEYS, PEER_HALF), PEER_HALF ** -0.5),
        'peer_u': nrm(30, (L, PEER_N, D_MODEL), D_MODEL ** -0.5),
        'peer_v': nrm(31, (L, PEER_N, D_MODEL), BETA),
        'ln2_g': 1.0 + nrm(32, (L, D_MODEL), 0.02),
        'ln2_b': nrm(33, (L, D_MODEL), 0.02),
    }

def reference(x_prompt, x_sample, cache_k, cache_v, state_wkv, state_shift, ln_in_g, ln_in_b,
              w_in, shift_mu, rw_w0, rw_w2, rw_a0, rw_a2, rw_g2, rw_kk, rw_ka, rw_rk, rw_lnx_g,
              rw_lnx_b, da_lq1, da_lk1, da_lq2, da_lk2, da_subln_g, w_out, ln1_g, ln1_b,
              peer_wq, peer_subkeys, peer_u, peer_v, ln2_g, ln2_b):
    pos_p = jnp.arange(x_prompt.shape[1])
    pos_s = PAST_LEN + jnp.arange(x_sample.shape[1])
    hp = _layer_norm(x_prompt, ln_in_g, ln_in_b)
    hs = _layer_norm(x_sample, ln_in_g, ln_in_b)
    bp = x_prompt.shape[0]
    kp_l, vp_l, sp_l, shp_l, ks_l, vs_l, ss_l, shs_l = [], [], [], [], [], [], [], []
    for l in range(DEPTH):
        lam_init = 0.8 - 0.6 * math.exp(-0.3 * l)

        def layer(h, pos, shift_prev, s0, ck, cv):
            m, nk, nv, ns, nsh = _mixer(h, pos, shift_prev, s0, ck, cv, w_in[l], shift_mu[l],
                                        rw_w0[l], rw_w2[l], rw_a0[l], rw_a2[l], rw_g2[l], rw_kk[l],
                                        rw_ka[l], rw_rk[l], rw_lnx_g[l], rw_lnx_b[l], da_lq1[l],
                                        da_lk1[l], da_lq2[l], da_lk2[l], da_subln_g[l], w_out[l],
                                        lam_init)
            h = _layer_norm(ALPHA * h + m, ln1_g[l], ln1_b[l])
            f = _peer(h, peer_wq[l], peer_subkeys[l], peer_u[l], peer_v[l])
            h = _layer_norm(ALPHA * h + f, ln2_g[l], ln2_b[l])
            return h, nk, nv, ns, nsh

        shift0 = jnp.zeros((bp, 1, RW_COLS), x_prompt.dtype)
        s_zero = jnp.zeros((bp, RW_HEADS, RW_HD, RW_HD), state_wkv.dtype)
        hp, kp, vp, sp, shp = layer(hp, pos_p, shift0, s_zero, None, None)
        hs, ksn, vsn, ssn, shsn = layer(hs, pos_s, state_shift[l], state_wkv[l], cache_k[l], cache_v[l])
        kp_l.append(kp); vp_l.append(vp); sp_l.append(sp); shp_l.append(shp)
        ks_l.append(ksn); vs_l.append(vsn); ss_l.append(ssn); shs_l.append(shsn)
    return (hp, hs, jnp.stack(kp_l), jnp.stack(vp_l), jnp.stack(sp_l), jnp.stack(shp_l),
            jnp.stack(ks_l), jnp.stack(vs_l), jnp.stack(ss_l), jnp.stack(shs_l))


_drawn_inputs = setup_inputs


def setup_inputs(seed=0):
    import zlib

    import numpy as np

    out = dict(_drawn_inputs(seed))
    spreads = {}
    factors = {'rw_lnx_g': 3.527,
     'rw_lnx_b': 3.21,
     'da_lk2': 8.0,
     'da_subln_g': 2.7,
     'ln2_g': 2.728,
     'ln2_b': 2.841}
    for name, (base, spread) in spreads.items():
        noise = np.random.default_rng([zlib.crc32(name.encode()), seed]).standard_normal(out[name].shape)
        drawn = base * np.exp(spread * noise) if base else spread * noise
        out[name] = __import__('jax').numpy.asarray(drawn.astype(out[name].dtype))
    for name, factor in factors.items():
        out[name] = (out[name] * factor).astype(out[name].dtype)
    return out
```

```python
from contextlib import ExitStack
import math

import numpy as np
import concourse.bass as bass
from concourse import mybir

F32 = mybir.dt.float32
I32 = mybir.dt.int32
U32 = mybir.dt.uint32
ALU = mybir.AluOpType
ACT = mybir.ActivationFunctionType
AX = mybir.AxisListType

P = 128
D = 1024
KT = D // P
SEQ, DEC, PAST = 1024, 64, 512
CH = 64
HD = 64
RW = 512
NJ = RW // P
RW_COLS = 1792
DA = 512
ROT = 16
THETA = 500000.0
DA_SCALE = HD ** -0.5
LAM_INIT = 0.8 - 0.6 * math.exp(-0.3 * 0)
ALPHA = 2.0 ** 0.25
LN_EPS, GN_EPS = 1e-5, 64e-5
DECAY = -math.exp(-0.5)
PH, NK, TOPK = 8, 128, 16
SLOTS = PH * TOPK
SEG = 256
NCH = SEG // CH
NT = SEG // P
PIECE = 8
RING = 2 * PIECE
ON_PE = 5
ITERS = SLOTS // RING
MU, W0, A0, KKW, KAW, RKW, LXG, LXB, SHIFT, SUBG = 0, 14, 18, 22, 26, 30, 34, 38, 42, 56
NPAR = 57
ROW_A, ROW_B = 4, 12
NCAND = ROW_A * TOPK + ROW_B * 4
LOW = -3.0e38


class Segment:
    def __init__(self, n, sample, start, width):
        self.n, self.sample, self.start, self.width = n, sample, start, width
        self.rows = min(width, P)
        self.tiles = (width + P - 1) // P
        self.chunks = width // CH
        self.last = sample or start + width == SEQ
        self.past = PAST if sample else start
        self.first_tile = 0 if n == 0 else 1 + (n - 1) * NT
        self.pos = (SEQ if sample else start)


SEGMENTS = [Segment(0, True, 0, DEC)] + [Segment(1 + i, False, i * SEG, SEG) for i in range(SEQ // SEG)]
TILES = [(s, t) for s in SEGMENTS for t in range(s.tiles)]


def mix_steps(s):
    steps = [("embed", s, 0)]
    for j in range(NJ):
        steps += [("rwkv", s, j), ("levels", s, j), ("chunks", s, j), ("attn", s, j)]
    steps += [("project", s, 0), ("query", s, 0)]
    steps += [("topk", s, t) for t in range(s.tiles)]
    return steps


def peer_steps(g, pieces):
    runs = [(a, min(a + pieces, ITERS)) for a in range(0, ITERS, pieces)]
    return ([("bring", g, None)] + [("u", g, r) for r in runs] + [("gate", g, None)]
            + [("v", g, r) for r in runs] + [("finish", g, None)])


def plan():
    steps = list(mix_steps(SEGMENTS[0]))
    for s in SEGMENTS:
        peers = [x for t in range(s.tiles) for x in peer_steps(s.first_tile + t, PIECES_A_STEP if s.n + 1 < len(SEGMENTS) else ITERS)]
        mixes = mix_steps(SEGMENTS[s.n + 1]) if s.n + 1 < len(SEGMENTS) else []
        if not OVERLAP:
            steps += peers + mixes
            continue
        done = 0
        for i, x in enumerate(peers):
            steps.append(x)
            upto = (i + 1) * len(mixes) // len(peers)
            steps += mixes[done:upto]
            done = upto
    return steps


OVERLAP = True
PIECES_A_STEP = 1


class Tally:

    def __init__(self, eng, own):
        self.eng, self.own, self.seen, self.made = eng, own, {}, 0

    def next(self, sem, n=1):
        self.seen[sem.name] = self.seen.get(sem.name, 0) + n
        self.eng.wait_ge(sem, self.seen[sem.name])

    def rounds(self, sem, n=1):
        if self.seen.get(sem.name, 0):
            self.eng.wait_ge(sem, self.seen[sem.name])
        self.seen[sem.name] = self.seen.get(sem.name, 0) + n

    def link(self, ins):
        self.made += 1
        ins.then_inc(self.own, 1)
        self.eng.wait_ge(self.own, self.made)

    def told(self, ins, sem):
        ins.then_inc(sem, 1)
        self.next(sem)


def build(nc, ins, outs):
    (y_p, y_s, k_p, v_p, wkv_p, sh_p, k_s, v_s, wkv_s, sh_s) = outs
    steps = plan()
    ctx = ExitStack()
    with ctx:
        def sb(name, shape, dt=F32):
            return ctx.enter_context(nc.sbuf_tensor(name, shape, dt))

        def sem(name):
            return ctx.enter_context(nc.semaphore(name))

        h_d = nc.dram_tensor("h_scratch", (SEG, D), F32, kind="Internal").ap()
        h1_d = nc.dram_tensor("h1_scratch", (len(TILES) * P, D), F32, kind="Internal").ap()
        kt_d = nc.dram_tensor("keys_scratch", (NJ, P, SEQ), F32, kind="Internal").ap()

        ident = sb("ident", [P, P])
        eye2 = sb("eye2", [P, HD])
        ones2 = sb("ones2", [P, P])
        mean2 = sb("mean2", [P, P])
        causal = sb("causal", [P, 2, CH])
        first_lo = sb("first_lo", [P, CH])
        lower = sb("lower", [P, 6, CH])
        restart = sb("restart", [P, SEG])
        iota16 = sb("iota16", [P, TOPK])
        zeros = sb("zeros", [P, P])
        eps_ln = sb("eps_ln", [P, 1])
        eps_gn = sb("eps_gn", [P, 1])
        par = sb("par", [P, NPAR])
        one_minus_ka = sb("one_minus_ka", [P, NJ])
        sub_scale = sb("sub_scale", [P, 1])
        neg_lam = sb("neg_lam", [P, 1])
        shift_rows = sb("shift_rows", [14, P])
        lam_sum = sb("lam_sum", [P, 2])
        lam_exp = sb("lam_exp", [P, 2])
        lora_wa = sb("lora_wa", [P, RW])
        lora_g = sb("lora_g", [P, RW])
        rope = sb("rope", [P, len(TILES), ROT])
        skT = sb("skT", [P, 2 * PH, NK])
        ln_mix = sb("ln_mix", [P, 2, D])
        ln2 = sb("ln2", [P, 2, D])

        hT = sb("hT", [P, KT, SEG])
        mixT = sb("mixT", [P, KT, SEG])
        wts = sb("wts", [P, 2, 3, KT, P])
        wl_al = sb("wl_al", [P, SEG])
        gate_in = sb("gate_in", [P, SEG])
        prev = sb("prev", [P, 2, 14])
        state = sb("state", [P, 2, NJ, HD])
        idx = sb("idx", [P, 2, NT, SLOTS], I32)
        gates = sb("gates", [P, 2, NT, SLOTS])

        ring = sb("ring", [P, RING, D])
        stage = sb("stage", [P, 2, PIECE], I32)
        h1 = sb("h1", [P, 2, D])
        dots8 = sb("dots8", [P, 2, PIECE])
        dots = sb("dots", [P, SLOTS])
        wgt = sb("wgt", [P, SLOTS])
        diag = sb("diag", [P, 2, ON_PE, P])
        acc = sb("acc", [P, D])
        st2 = sb("st2", [P, 2, 6])
        mv2 = sb("mv2", [P, 2])
        sd2 = sb("sd2", [P, 1])

        ARENA = 10560
        arena = sb("arena", [P, ARENA])
        top = [0]

        def carve(*shape):
            n = int(np.prod(shape))
            a = arena[:, top[0]:top[0] + n]
            top[0] += n
            assert top[0] <= ARENA, top[0]
            if len(shape) == 1:
                return a
            names = "abcd"[:len(shape)]
            kw = {c: v for c, v in zip(names[1:], shape[1:])}
            return a.rearrange(f"p ({' '.join(names)}) -> p {' '.join(names)}", **kw)

        x_in = carve(NT, D)
        st1 = carve(2, 6)
        mv1 = carve(2)
        sd1 = carve(1)
        raw2 = carve(2, SEG + 1)
        dif = carve(SEG)
        top[0] = 0
        raw = carve(3, SEG + 1)
        rkv = carve(3, SEG)
        delta = carve(SEG)
        lw = carve(SEG)
        cum = carve(SEG)
        cumx = carve(SEG)
        a_t = carve(SEG)
        g_t = carve(SEG)
        dec_i = carve(SEG)
        dec_x = carve(SEG)
        dec_n = carve(SEG)
        kk = carve(SEG)
        sq = carve(SEG)
        nrm = carve(SEG)
        rkk = carve(SEG)
        kr = carve(NCH, 2, CH)
        kt = carve(SEG)
        bt = carve(SEG)
        bonus = carve(SEG)
        lt_ab = carve(NCH, 2, CH)
        mk_ak = carve(NCH, 2, CH)
        xm = carve(NCH, CH)
        xt = carve(NCH, CH)
        zs = carve(NCH, CH)
        joins = carve(5, NCH, CH)
        tok = carve(3, NCH, CH)
        p1s = carve(HD)
        us = carve(HD)
        s_dec = carve(HD)
        yraw = carve(SEG)
        s_out = carve(HD)
        top[0] = 0
        keysT = carve(SEQ)
        vals = carve(KT, P)
        qT = carve(SEG)
        qk = carve(NT, 2 * P)
        old_k = carve(4, P)
        r1 = carve(4, 8)
        r2 = carve(4, 8)
        r3 = carve(4, 8)
        r4 = carve(4, 8)
        probs = carve(2, SEQ)
        attT = carve(KT, P)
        mx = carve(2)
        negm = carve(2)
        zsum = carve(2)
        rz = carve(2)
        ratio = carve(1)
        o_s = carve(P)
        o_sq = carve(P)
        ss = carve(1)
        rms = carve(1)
        top[0] = 0
        x1 = carve(NT, D)
        st3 = carve(2, 6)
        mv3 = carve(2)
        sd3 = carve(1)
        qsT = carve(2, SEG)
        top[0] = 3000
        scores = carve(NT, 2 * PH, NK)
        v16 = carve(2 * PH, TOPK)
        i16f = carve(2 * PH, TOPK)
        work = carve(NK)
        t16 = carve(PH, TOPK)
        pos_f = carve(PH, TOPK)
        af = carve(PH, TOPK)
        bf = carve(PH, TOPK)
        e1 = carve(PH, TOPK)
        e2 = carve(PH, TOPK)
        hmax = carve(PH)
        top[0] = 0
        cand = carve(PH, NCAND)
        hot = carve(SLOTS, TOPK)
        top[0] = 8600
        i16 = carve(2 * PH, TOPK).bitcast(U32)
        pos = carve(PH, TOPK).bitcast(U32)
        posb = carve(4, PH * TOPK).bitcast(U32)
        top[0] = 9600
        lam_in = carve(4, HD)
        lam_work = carve(HD)

        pm = ctx.enter_context(nc.psum_tensor("pm", [P, 6, 512], F32))
        pacc = ctx.enter_context(nc.psum_tensor("pacc", [P, 2, 512], F32))

        names = """own_dve own_act own_pool own_pe bar_sp bar_pool bar_act bar_pe bar_dve par_in par_full consts
            sub_full sub_read lam_ready lam_exp_ready x_in0 x_in1 w0 w1 h_stored mv sd h_ready t_full t_read
            lora_full lora_read lora_mixed raw_full raw_read lo_full lo_sig cum_ready exps sq_ready n2_full
            nrm_ready kr_ready g_full masked bon_full tok_full tok_read join_ready x_ready z_full z_read
            xz_full x_new p1_full p1_read u_full u_read s_full st_new y_full y_read mean_full ysq_ready var_full
            ysd out_full out_read st_stored hist old_full old_read qkv_full qkv_read roped kv_stored qkT_full
            qkT_read kt_stored sc_full max_ready prob_ready att_ready attT_full attT_read o_full o_read o_ready
            oT_full oT_read rms_ready res_in wset m_read q_full q_read qs_full qs_read h1_stored idx_ready
            shift_full shift_read shift_stored staged parked peer_dve peer_pe dot_kept u_done gelu_done
            weight_ready diag_ready acc_made f_ready f_read mv2s sd2s y_ready y_stored h1_in0 h1_in1 lnm_in
            max_exp exp_ready rwkv_init init_done topk_done""".split()
        S = {n: sem(n) for n in names}
        s_row = [sem(f"row{r}") for r in range(RING)]

        block = ctx.enter_context(nc.Block())

        PHASE_OF = {}
        for st in steps:
            if st[0] in ("embed", "rwkv", "attn", "project"):
                PHASE_OF[(st[0], st[1].n, st[2])] = len(PHASE_OF)
        PHASE_LIST = sorted(PHASE_OF, key=PHASE_OF.get)

        def enter(eng, me, kind, s, j):
            n = PHASE_OF[(kind, s.n, j)] + 1
            for other in ("sp", "pool", "act", "pe", "dve"):
                if other != me:
                    eng.wait_ge(S["bar_" + other], n)

        def leave(eng, me):
            eng.drain().then_inc(S["bar_" + me], 1)

        def sl(s, t):
            return slice(t * P, t * P + s.rows)

        def cols(s, c):
            return slice(c * CH, c * CH + CH)

        def halves():
            return (slice(0, HD), slice(HD, P))

        def x_rows(s, t):
            src = ins["x_sample"] if s.sample else ins["x_prompt"]
            return src[0, s.start + t * P:s.start + t * P + s.rows, :]

        w_in = ins["w_in"][0].rearrange("(k p) n -> p k n", p=P)
        w_out = ins["w_out"][0].rearrange("(k p) n -> p k n", p=P)
        w_q = ins["peer_wq"][0].rearrange("(k p) n -> p k n", p=P)

        def piece(kind, j):
            if kind == "embed":
                return [w_in[:, :, 3 * RW:3 * RW + P], w_in[:, :, 3 * RW + P:3 * RW + 2 * P]]
            if kind == "rwkv":
                return [w_in[:, :, x * RW + j * P:x * RW + (j + 1) * P] for x in (0, 1, 2)]
            if kind == "attn":
                return [w_in[:, :, RW_COLS + x * DA + j * P:RW_COLS + x * DA + (j + 1) * P] for x in (0, 1, 2)]
            w = w_out if kind == "out" else w_q
            n = KT if kind == "out" else 2 * PH
            return [w[:, :, i * P:(i + 1) * P] for i in range(3 * j, min(3 * j + 3, n))]

        SETS = []
        for kind, n, j in PHASE_LIST:
            if kind == "project":
                SETS += [("out", i) for i in range(3)] + [("q", i) for i in range(6)]
            else:
                SETS.append((kind, j))
        PER_SEG = 2 * NJ + 1 + 9

        def set_number(kind, s, j):
            base = s.n * PER_SEG
            return base + {"embed": 0, "rwkv": 1 + 2 * j, "attn": 2 + 2 * j, "out": 2 * NJ + 1 + j,
                           "q": 2 * NJ + 4 + j}[kind]

        def weights_in(k):
            return 16 * sum(len(piece(*SETS[i])) for i in range(k % 2, k + 1, 2))

        @block.sync
        def _(sp):
            tl = Tally(sp, None)
            loaded = [0]

            def load_set(k):
                if k < len(SETS):
                    for i, w in enumerate(piece(*SETS[k])):
                        sp.dma_start(wts[:, k % 2, i], w).then_inc(S[f"w{k % 2}"], 16)

            row = x_in[:, 0, 0:P]
            rows = [(MU, "shift_mu", 14), (W0, "rw_w0", 4), (A0, "rw_a0", 4), (KKW, "rw_kk", 4), (KAW, "rw_ka", 4),
                    (RKW, "rw_rk", 4), (LXG, "rw_lnx_g", 4), (LXB, "rw_lnx_b", 4), (SUBG, "da_subln_g", 1)]
            for at, name, n in rows:
                src = ins[name][0]
                if name == "rw_rk":
                    src = src.rearrange("h d -> (h d)")
                sp.dma_start(row[at:at + n, :], src.rearrange("(c p) -> c p", p=P)).then_inc(S["par_in"], 16)
            sp.dma_start(row[SHIFT:SHIFT + 14, :],
                         ins["state_shift"][0, 0, 0].rearrange("(c p) -> c p", p=P)).then_inc(S["par_in"], 16)
            load_set(0)
            sp.dma_start(lora_wa[0:64, :], ins["rw_w2"][0]).then_inc(S["par_in"], 16)
            sp.dma_start(lora_wa[64:128, :], ins["rw_a2"][0]).then_inc(S["par_in"], 16)
            sp.dma_start(lora_g[:, :], ins["rw_g2"][0]).then_inc(S["par_in"], 16)
            for i, name in enumerate(("da_lq1", "da_lk1", "da_lq2", "da_lk2")):
                sp.dma_start(lam_in[:, i, :], ins[name][0].partition_broadcast(P)).then_inc(S["par_in"], 16)
            for i, name in enumerate(("ln2_g", "ln2_b")):
                sp.dma_start(ln2[:, i, :], ins[name][0].partition_broadcast(P)).then_inc(S["par_in"], 16)
            sp.dma_start(rope[:, 1:, :], ins["rope"][0:SEQ].rearrange("(t p) c -> p t c", p=P)).then_inc(S["par_in"], 16)
            sp.dma_start(rope[0:DEC, 0, :], ins["rope"][SEQ:SEQ + DEC]).then_inc(S["par_in"], 16)
            sp.dma_start(scores[:, 0], ins["peer_subkeys"][0].rearrange("h c n d -> n (h c) d")).then_inc(S["par_in"], 16)
            for e in range(1):
                sp.dma_start(x_in[:, 1, 0:NJ * HD].rearrange("p (j k) -> p j k", j=NJ),
                             ins["state_wkv"][0, 0].rearrange("(j e) v k -> (e v) j k", e=2)).then_inc(S["par_in"], 16)
            sp.wait_ge(S["init_done"], 1)
            sp.sem_inc(S["bar_sp"], 1)

            for kind, s, j in steps:
                out_k, out_v = (k_s, v_s) if (s in SEGMENTS and s.sample) else (k_p, v_p)
                if kind == "embed":
                    enter(sp, "sp", kind, s, j)
                    load_set(set_number("embed", s, 0) + 1)
                    for i, name in enumerate(("ln_in_g", "ln_in_b")):
                        sp.dma_start(ln_mix[:, i, :], ins[name].partition_broadcast(P)).then_inc(S["lnm_in"], 16)
                    for t in range(s.tiles):
                        sp.dma_start(x_in[0:s.rows, t, :], x_rows(s, t)).then_inc(S[f"x_in{t}"], 16)
                    for t in range(s.tiles):
                        tl.next(S["h_ready"])
                        sp.dma_start(h_d[t * P:t * P + s.rows, :], x_in[0:s.rows, t, :]).then_inc(S["h_stored"], 16)
                    tl.next(S["h_stored"], 16 * s.tiles)
                    sp.sem_inc(S["bar_sp"], 1)
                elif kind == "rwkv":
                    enter(sp, "sp", kind, s, j)
                    load_set(set_number("rwkv", s, j) + 1)
                elif kind == "chunks":
                    if s.last:
                        tl.next(S["out_read"])
                        dst = wkv_s if s.sample else wkv_p
                        sp.dma_start(dst[0, 0, 2 * j:2 * j + 2].rearrange("h v k -> (h v) k"), s_out).then_inc(S["st_stored"], 16)
                        tl.next(S["st_stored"], 16)
                    sp.sem_inc(S["bar_sp"], 1)
                elif kind == "attn":
                    enter(sp, "sp", kind, s, j)
                    if s.sample:
                        sp.dma_start(old_k, ins["cache_k"][0, 0, :, j, :].rearrange("(b p) e -> p b e", p=P)).then_inc(S["hist"], 16)
                        sp.dma_start(vals[:, 0:PAST // P], ins["cache_v"][0, 0, :, j, :].rearrange("(b p) e -> p b e", p=P)).then_inc(S["hist"], 16)
                    elif s.past:
                        sp.dma_start(keysT[:, 0:s.past], kt_d[j, :, 0:s.past]).then_inc(S["hist"], 16)
                        sp.dma_start(vals[:, 0:s.past // P], v_p[0, 0, 0:s.past, j, :].rearrange("(b p) e -> p b e", p=P)).then_inc(S["hist"], 16)
                    load_set(set_number("attn", s, j) + 1)
                    for t in range(s.tiles):
                        tl.next(S["roped"])
                        r = slice(s.start + t * P, s.start + t * P + s.rows)
                        sp.dma_start(out_k[0, 0, r, j, :], qk[0:s.rows, t, P:2 * P]).then_inc(S["kv_stored"], 16)
                        sp.dma_start(out_v[0, 0, r, j, :], vals[0:s.rows, s.past // P + t, :]).then_inc(S["kv_stored"], 16)
                    tl.next(S["kv_stored"], 32 * s.tiles)
                    tl.next(S["qkT_read"], 2 * s.tiles)
                    if not s.sample:
                        sp.dma_start(kt_d[j, :, s.past:s.past + s.width], keysT[:, s.past:s.past + s.width]).then_inc(S["kt_stored"], 16)
                        tl.next(S["kt_stored"], 16)
                    sp.sem_inc(S["bar_sp"], 1)
                elif kind == "project":
                    enter(sp, "sp", kind, s, j)
                    for i, name in enumerate(("ln1_g", "ln1_b")):
                        sp.dma_start(ln_mix[:, i, :], ins[name][0].partition_broadcast(P)).then_inc(S["lnm_in"], 16)
                    for t in range(s.tiles):
                        sp.dma_start(x1[0:s.rows, t, :], h_d[t * P:t * P + s.rows, :]).then_inc(S["res_in"], 16)
                    base = set_number("out", s, 0)
                    load_set(base + 1)
                    for i in range(3):
                        tl.next(S["wset"])
                        load_set(base + i + 2)
                    for t in range(s.tiles):
                        tl.next(S["h_ready"])
                        g = s.first_tile + t
                        sp.dma_start(h1_d[g * P:g * P + s.rows, :], x1[0:s.rows, t, :]).then_inc(S["h1_stored"], 16)
                    tl.next(S["h1_stored"], 16 * s.tiles)
                elif kind == "query":
                    base = set_number("q", s, 0)
                    for i in range(6):
                        n = len(piece("q", i))
                        tl.next(S["q_full"], n)
                        if i >= 0 and i < 5:
                            load_set(base + i + 2)
                    sp.sem_inc(S["bar_sp"], 1)
                    if s.last:
                        dst = sh_s if s.sample else sh_p
                        tl.next(S["shift_read"])
                        sp.dma_start(dst[0, 0, 0].rearrange("(c p) -> c p", p=P), shift_rows[:, :]).then_inc(S["shift_stored"], 16)
                elif kind == "bring":
                    g = s
                    seg, t = TILES[g]
                    if g >= 2:
                        sp.wait_ge(S["y_stored"], 16 * (g - 1))
                    sp.dma_start(h1[0:seg.rows, g % 2, :], h1_d[g * P:g * P + seg.rows, :]).then_inc(S[f"h1_in{g % 2}"], 16)
                elif kind == "finish":
                    g = s
                    seg, t = TILES[g]
                    tl.next(S["y_ready"])
                    dst = y_s if seg.sample else y_p
                    r = slice(seg.start + t * P, seg.start + t * P + seg.rows)
                    sp.dma_start(dst[0, r, :], h1[0:seg.rows, g % 2, :]).then_inc(S["y_stored"], 16)
            sp.wait_ge(S["y_stored"], 16 * len(TILES))
            sp.wait_ge(S["shift_stored"], 32)

        @block.gpsimd
        def _(pool):
            tl = Tally(pool, S["own_pool"])
            tl.link(pool.memset(ident[:, :], 0.0))
            tl.link(pool.affine_select(out=ident[:, :], in_=ident[:, :], compare_op=ALU.not_equal, fill=1.0, base=0,
                                       pattern=[[-1, P]], channel_multiplier=1))
            tl.link(pool.memset(zeros[:, :], 0.0))
            tl.link(pool.memset(ones2[:, :], 0.0))
            tl.link(pool.memset(mean2[:, :], 0.0))
            for h in halves():
                tl.link(pool.memset(ones2[h, h], 1.0))
                tl.link(pool.memset(mean2[h, h], 1.0 / HD))
            tl.link(pool.memset(causal[:, :, :], 1.0))
            tl.link(pool.memset(lower[:, :, :], 1.0))
            tl.link(pool.memset(first_lo[:, :], 1.0))
            tl.link(pool.memset(restart[:, :], 1.0))
            tl.link(pool.memset(restart[:, 0:SEG:CH], 0.0))
            tl.link(pool.memset(eps_ln[:, :], LN_EPS))
            tl.link(pool.memset(eps_gn[:, :], GN_EPS))
            tl.link(pool.memset(prev[:, :, :], 0.0))
            tl.link(pool.memset(state[:, :, :, :], 0.0))
            tl.link(pool.iota(iota16[:, :], pattern=[[1, TOPK]], base=0, channel_multiplier=0,
                              allow_small_or_imprecise_dtypes=True))

            def keep(out, pattern, base, mult, op=ALU.is_ge):
                tl.link(pool.affine_select(out=out, in_=out, compare_op=op, fill=0.0, base=base, pattern=pattern,
                                           channel_multiplier=mult))
            for h in halves():
                keep(causal[h, 0, :], [[1, CH]], -1, -1)
                keep(causal[h, 1, :], [[1, CH]], 0, -1)
                for l in range(6):
                    w = 1 << l
                    v = lower[h, l, :].rearrange("p (a b c) -> p a b c", b=2, c=w)
                    pat = [[-2 * w, CH // (2 * w)], [0, 2], [0, w]]
                    neg = [[2 * w, CH // (2 * w)], [0, 2], [0, w]]
                    keep(v, pat, 0, 1)
                    keep(v, neg, w - 1, -1)
                    keep(v, [[0, CH // (2 * w)], [1, 2], [0, w]], -1, 0)
                v = first_lo[h, :].rearrange("p (a b) -> p a b", b=2)
                keep(v, [[-2, CH // 2], [-1, 2]], -1, 1, ALU.is_equal)
                keep(v, [[0, CH // 2], [-1, 2]], 0, 0)
            pool.drain().then_inc(S["consts"], 1)
            pool.wait_ge(S["init_done"], 1)
            pool.sem_inc(S["bar_pool"], 1)

            def gather(table, g, seg, t, i, half, turn, pe_need):
                pool.wait_ge(S["peer_dve"], turn)
                pool.sem_inc(S["parked"], 1)
                pool.wait_ge(S["peer_pe"], pe_need)
                pool.sem_inc(S["parked"], 1)
                pool.tensor_copy(stage[0:seg.rows, half, :],
                                 idx[0:seg.rows, seg.n % 2, t, bass.ds(i * RING + half * PIECE, PIECE)]).then_inc(S["staged"], 1)
                pool.wait_ge(S["staged"], turn)
                pool.sem_inc(S["parked"], 1)
                for r in range(PIECE):
                    pool.indirect_dma_start(
                        out=ring[0:seg.rows, half * PIECE + r, :], out_offset=None, in_=table,
                        in_offset=bass.IndirectOffsetOnAxis(ap=stage[0:seg.rows, half, r:r + 1].bitcast(U32), axis=0)
                    ).then_inc(s_row[half * PIECE + r], 16)

            for kind, s, j in steps:
                if kind in ("embed", "attn"):
                    enter(pool, "pool", kind, s, j)
                    pool.sem_inc(S["bar_pool"], 1)
                elif kind == "rwkv":
                    enter(pool, "pool", kind, s, j)
                elif kind == "levels":
                    tl.next(S["masked"])
                    for l in range(1, 6):
                        pool.tensor_tensor(joins[:, l - 1, 0:s.chunks, :], lt_ab[:, 0:s.chunks, 0, :],
                                           lower[:, l, None, :].to_broadcast([P, s.chunks, CH]), ALU.mult
                                           ).then_inc(S["join_ready"], 1)
                elif kind == "chunks":
                    leave(pool, "pool")
                elif kind == "project":
                    enter(pool, "pool", kind, s, j)
                    pool.sem_inc(S["bar_pool"], 1)
                elif kind == "bring":
                    seg, t = TILES[s]
                    if t == 0:
                        pool.wait_ge(S["idx_ready"], s + seg.tiles)
                elif kind in ("u", "v"):
                    g, (a, b) = s, j
                    seg, t = TILES[g]
                    table = (ins["peer_u"] if kind == "u" else ins["peer_v"])[0]

                    def turn_of_ring(i):
                        for half in range(2):
                            n = 4 * ITERS * g + (2 * ITERS if kind == "v" else 0) + half
                            pe = 2 * ITERS * g + 1 + half if kind == "u" else 2 * ITERS * g + half + 1 + i * 2
                            gather(table, g, seg, t, i, half, i * 2 + n + 1, pe)
                    if b - a == 1:
                        turn_of_ring(a)
                    else:
                        with pool.Fori(a, b) as i:
                            turn_of_ring(i)

        @block.scalar
        def _(act):
            tl = Tally(act, S["own_act"])
            act.wait_ge(S["consts"], 1)
            tl.next(S["par_full"])
            tl.link(act.activation(par[:, :], pm[:, 0, 0:NPAR], ACT.Copy))
            tl.link(act.activation(prev[:, 1, :], par[:, SHIFT:SHIFT + 14], ACT.Copy))
            for i in range(4):
                tl.next(S["sub_full"])
                tl.link(act.activation(skT[:, 4 * i:4 * i + 4, :], pm[:, 1 + i, :].rearrange("p (c n) -> p c n", n=NK), ACT.Copy))
            tl.next(S["sub_full"])
            tl.link(act.activation(state[:, 1, :, :], pm[:, 5, 0:NJ * HD].rearrange("p (j v) -> p j v", j=NJ), ACT.Copy))
            tl.next(S["lam_ready"])
            act.activation(lam_exp[:, :], lam_sum[:, :], ACT.Exp).then_inc(S["lam_exp_ready"], 1)
            act.wait_ge(S["lam_exp_ready"], 1)
            act.wait_ge(S["init_done"], 1)
            act.sem_inc(S["bar_act"], 1)

            def diagonals(g, seg, i):
                for half in range(2):
                    act.wait_ge(S["peer_pe"], i * 2 + half + 1 + 2 * ITERS * g)
                    for r in range(ON_PE):
                        x = act.activation(diag[0:seg.rows, half, r, 0:seg.rows], ident[0:seg.rows, 0:seg.rows], ACT.Copy,
                                           scale=wgt[0:seg.rows, bass.ds(i * RING + half * PIECE + r, 1)])
                    x.then_inc(S["diag_ready"], 1)

            for kind, s, j in steps:
                if kind == "embed":
                    enter(act, "act", kind, s, j)
                    for t in range(s.tiles):
                        tl.next(S["mv"])
                        act.activation(sd1[0:s.rows], mv1[0:s.rows, 1:2], ACT.Sqrt, bias=eps_ln[0:s.rows, :]).then_inc(S["sd"], 1)
                        for i in range(2):
                            tl.next(S["t_full"])
                            act.activation(hT[:, 4 * i:4 * i + 4, sl(s, t)],
                                           pm[:, i, :].rearrange("p (k n) -> p k n", n=P)[:, :, 0:s.rows],
                                           ACT.Copy).then_inc(S["t_read"], 1)
                    for x in range(2):
                        tl.next(S["lora_full"])
                        act.activation(raw2[:, x, 1:1 + s.width], pm[:, 2 + x, 0:s.width], ACT.Copy).then_inc(S["lora_read"], 1)
                    tl.next(S["lora_mixed"])
                    act.activation(wl_al[0:64, 0:s.width], wl_al[0:64, 0:s.width], ACT.Tanh)
                    act.activation(gate_in[:, 0:s.width], gate_in[:, 0:s.width], ACT.Sigmoid)
                    leave(act, "act")
                elif kind == "rwkv":
                    enter(act, "act", kind, s, j)
                    w = s.width
                    for x in (1, 0, 2):
                        tl.next(S["raw_full"])
                        act.activation(raw[:, x, 1:1 + w], pm[:, x, 0:w], ACT.Copy).then_inc(S["raw_read"], 1)
                    tl.next(S["lo_full"])
                    act.activation(lw[:, 0:w], pm[:, 3, 0:w], ACT.Sigmoid, bias=par[:, W0 + j:W0 + j + 1]).then_inc(S["lo_sig"], 1)
                    tl.next(S["lo_full"])
                    act.activation(a_t[:, 0:w], pm[:, 4, 0:w], ACT.Sigmoid, bias=par[:, A0 + j:A0 + j + 1]).then_inc(S["lo_sig"], 1)
                    tl.next(S["lo_full"])
                    act.activation(g_t[:, 0:w], pm[:, 5, 0:w], ACT.Copy).then_inc(S["lo_sig"], 1)
                    tl.next(S["cum_ready"])
                    act.activation(dec_i[:, 0:w], cum[:, 0:w], ACT.Exp)
                    act.activation(dec_n[:, 0:w], cum[:, 0:w], ACT.Exp, scale=-1.0)
                    act.activation(dec_x[:, 0:w], cumx[:, 0:w], ACT.Exp).then_inc(S["exps"], 1)
                    tl.next(S["n2_full"])
                    act.activation(nrm[:, 0:w], pm[:, 0, 0:w], ACT.Sqrt).then_inc(S["nrm_ready"], 1)
                    tl.next(S["tok_full"])
                    act.activation(tok[:, 0:2, 0:s.chunks, :],
                                   pm[:, 5, :].rearrange("p (x c n) -> p x c n", x=2, c=NCH)[:, :, 0:s.chunks, :],
                                   ACT.Copy).then_inc(S["tok_read"], 1)
                    tl.next(S["tok_full"])
                    act.activation(tok[:, 2, 0:s.chunks, :], pm[:, 0, 0:w].rearrange("p (c n) -> p c n", n=CH),
                                   ACT.Copy).then_inc(S["tok_read"], 1)
                elif kind == "levels":
                    for l in range(1, 6):
                        tl.next(S["z_full"])
                        act.activation(zs[:, 0:s.chunks, :], pm[:, 1, 0:s.width].rearrange("p (c n) -> p c n", n=CH),
                                       ACT.Copy).then_inc(S["z_read"], 1)
                elif kind == "chunks":
                    w = s.width
                    tl.next(S["y_full"])
                    act.activation(yraw[:, 0:w], pm[:, 5, 0:w], ACT.Copy).then_inc(S["y_read"], 1)
                    tl.next(S["var_full"])
                    act.activation(nrm[:, 0:w], pm[:, 4, 0:w], ACT.Sqrt, bias=eps_gn[:, :]).then_inc(S["ysd"], 1)
                    if s.last:
                        tl.next(S["out_full"])
                        act.activation(s_out, pm[:, 0, 0:HD], ACT.Copy).then_inc(S["out_read"], 1)
                    leave(act, "act")
                elif kind == "attn":
                    enter(act, "act", kind, s, j)
                    if s.sample:
                        tl.next(S["old_full"])
                        act.activation(keysT[:, 0:PAST], pm[:, 4, :], ACT.Copy).then_inc(S["old_read"], 1)
                    for t in range(s.tiles):
                        tl.next(S["qkv_full"])
                        act.activation(qk[0:s.rows, t, :], pm[0:s.rows, t, 0:2 * P], ACT.Copy)
                        act.activation(vals[0:s.rows, s.past // P + t, :], pm[0:s.rows, t, 2 * P:3 * P],
                                       ACT.Copy).then_inc(S["qkv_read"], 1)
                    for t in range(s.tiles):
                        tl.next(S["qkT_full"])
                        act.activation(qT[:, sl(s, t)], pm[:, 2 + t, 0:s.rows], ACT.Copy).then_inc(S["qkT_read"], 1)
                        act.activation(keysT[:, s.past + t * P:s.past + t * P + s.rows], pm[:, 2 + t, P:P + s.rows],
                                       ACT.Copy).then_inc(S["qkT_read"], 1)
                    for t in range(s.tiles):
                        r, nk = s.rows, s.past + t * P + s.rows
                        tl.next(S["max_ready"])
                        for c in range(2):
                            x = act.activation(probs[0:r, c, 0:nk], pm[0:r, 2 * c:2 * c + 2, :].rearrange("p a n -> p (a n)")[:, 0:nk],
                                               ACT.Exp, bias=negm[0:r, c:c + 1], scale=DA_SCALE, accum_out=zsum[0:r, c:c + 1])
                        x.then_inc(S["prob_ready"], 1)
                        nb = (nk + P - 1) // P
                        for b in range((nb + 3) // 4):
                            tl.next(S["attT_full"])
                            n = min(4, nb - 4 * b)
                            full = n if nk >= (4 * b + n) * P else n - 1
                            if full:
                                x = act.activation(attT[:, 4 * b:4 * b + full, 0:r],
                                                   pm[:, 4 + b, :].rearrange("p (k n) -> p k n", n=P)[:, 0:full, 0:r], ACT.Copy)
                            if full < n:
                                k = nk % P
                                x = act.activation(attT[0:k, 4 * b + full, 0:r], pm[0:k, 4 + b, full * P:full * P + r], ACT.Copy)
                            x.then_inc(S["attT_read"], 1)
                        tl.next(S["o_full"])
                        tl.link(act.activation(o_s[0:r], pm[0:r, 0, 0:P], ACT.Copy, scale=rz[0:r, 0:1]))
                        tl.link(act.activation(o_sq[0:r], o_s[0:r], ACT.Square, accum_out=ss[0:r]))
                        act.activation(rms[0:r], ss[0:r], ACT.Sqrt, bias=eps_ln[0:r, :], scale=1.0 / P).then_inc(S["rms_ready"], 1)
                        tl.next(S["oT_full"])
                        act.activation(mixT[:, NJ + j, sl(s, t)], pm[:, 1, 0:r], ACT.Copy, scale=sub_scale[:, :]).then_inc(S["oT_read"], 1)
                    leave(act, "act")
                elif kind == "project":
                    enter(act, "act", kind, s, j)
                    for t in range(s.tiles):
                        tl.next(S["mv"])
                        act.activation(sd3[0:s.rows], mv3[0:s.rows, 1:2], ACT.Sqrt, bias=eps_ln[0:s.rows, :]).then_inc(S["sd"], 1)
                        for i in range(2):
                            tl.next(S["t_full"])
                            act.activation(hT[:, 4 * i:4 * i + 4, sl(s, t)],
                                           pm[:, 4 + i, :].rearrange("p (k n) -> p k n", n=P)[:, :, 0:s.rows],
                                           ACT.Copy).then_inc(S["t_read"], 1)
                elif kind == "query":
                    for c in range(2 * PH):
                        tl.next(S["q_full"])
                        if c >= 2:
                            act.wait_ge(S["qs_full"], s.n * 2 * PH + c - 1)
                        act.activation(qsT[:, c % 2, 0:s.width], pm[:, c % 2, 0:s.width], ACT.Copy).then_inc(S["q_read"], 1)
                        if c % 4 == 3:
                            act.wait_ge(S["qs_full"], s.n * 2 * PH + c + 1)
                            for t in range(s.tiles):
                                x = act.activation(scores[0:s.rows, t, c - 3:c + 1, :],
                                                   pm[0:s.rows, 2 + t, :].rearrange("p (c n) -> p c n", n=NK), ACT.Copy)
                            x.then_inc(S["qs_read"], 1)
                    if s.last:
                        if not s.sample:
                            act.wait_ge(S["shift_stored"], 16)
                        tl.next(S["shift_full"])
                        act.activation(shift_rows[:, :], pm[0:14, 4, 0:P], ACT.Copy).then_inc(S["shift_read"], 1)
                elif kind == "topk":
                    tl.next(S["max_exp"])
                    act.activation(t16[0:s.rows], t16[0:s.rows], ACT.Exp).then_inc(S["exp_ready"], 1)
                    if j == s.tiles - 1:
                        leave(act, "act")
                elif kind == "gate":
                    seg, t = TILES[s]
                    act.wait_ge(S["dot_kept"], 2 * ITERS * (s + 1) + 2)
                    act.activation(dots[0:seg.rows, :], dots[0:seg.rows, :], ACT.Gelu).then_inc(S["gelu_done"], 1)
                elif kind == "v":
                    g, (a, b) = s, j
                    seg, t = TILES[g]
                    act.wait_ge(S["weight_ready"], g + 1)
                    if b - a == 1:
                        diagonals(g, seg, a)
                    else:
                        with act.Fori(a, b) as i:
                            diagonals(g, seg, i)
                elif kind == "finish":
                    seg, t = TILES[s]
                    tl.next(S["mv2s"])
                    act.activation(sd2[0:seg.rows, :], mv2[0:seg.rows, 1:2], ACT.Sqrt, bias=eps_ln[0:seg.rows, :]).then_inc(S["sd2s"], 1)

        @block.tensor
        def _(pe):
            tl = Tally(pe, S["own_pe"])
            pe.wait_ge(S["consts"], 1)
            pe.wait_ge(S["par_in"], 16 * 23)
            pe.transpose(pm[:, 0, 0:NPAR], x_in[0:NPAR, 0, 0:P], ident[0:NPAR, 0:NPAR]).then_inc(S["par_full"], 1)
            for i in range(4):
                for c in range(4):
                    x = pe.transpose(pm[:, 1 + i, c * NK:(c + 1) * NK], scores[:, 0, 4 * i + c, :], ident[:, :])
                x.then_inc(S["sub_full"], 1)
            for j in range(NJ):
                for h in halves():
                    x = pe.matmul(pm[h, 5, j * HD:(j + 1) * HD], x_in[h, 1, j * HD:(j + 1) * HD], ident[h, h], start=True, stop=True)
            x.then_inc(S["sub_full"], 1)
            pe.wait_ge(S["init_done"], 1)
            pe.sem_inc(S["bar_pe"], 1)

            def dense(out, lhs, rhs):
                for k in range(KT):
                    x = pe.matmul(out, lhs(k), rhs(k), start=(k == 0), stop=(k == KT - 1))
                return x

            def transpose_tile(s, t, src, bank):
                for i in range(2):
                    if t > 0:
                        tl.next(S["t_read"])
                    for k in range(4):
                        x = pe.transpose(pm[:, bank + i, k * P:k * P + s.rows], src[0:s.rows, t, (4 * i + k) * P:(4 * i + k + 1) * P],
                                         ident[0:s.rows, 0:s.rows])
                    x.then_inc(S["t_full"], 1)

            def per_head(bank, col, width, lhs, rhs, start=True, stop=True):
                for h in halves():
                    x = pe.matmul(pm[h, bank, col:col + width], lhs[h], rhs[h], start=start, stop=stop, skip_group_check=True)
                return x

            def sum_rows(g, seg, i):
                r = slice(0, seg.rows)
                for half in range(2):
                    pe.wait_ge(S["diag_ready"], i * 2 + half + 1 + 2 * ITERS * g)
                    for n in range(ON_PE):
                        slot = half * PIECE + n
                        pe.wait_ge(s_row[slot], i * 16 + 16 * (2 * ITERS * g + ITERS + 1))
                        for c in range(2):
                            x = pe.matmul(pacc[r, c, :], diag[r, half, n, r], ring[r, slot, c * 512:(c + 1) * 512],
                                          start=False, stop=False, skip_group_check=True)
                    x.then_inc(S["peer_pe"], 1)

            for kind, s, j in steps:
                if kind == "embed":
                    enter(pe, "pe", kind, s, j)
                    k0 = set_number("embed", s, 0)
                    for t in range(s.tiles):
                        tl.next(S["h_ready"])
                        transpose_tile(s, t, x_in, 0)
                    tl.next(S["t_read"], 2)
                    pe.wait_ge(S[f"w{k0 % 2}"], weights_in(k0))
                    for x in range(2):
                        dense(pm[:, 2 + x, 0:s.width], lambda k: wts[:, k0 % 2, x, k, :], lambda k: hT[:, k, 0:s.width]
                              ).then_inc(S["lora_full"], 1)
                    leave(pe, "pe")
                elif kind == "rwkv":
                    enter(pe, "pe", kind, s, j)
                    w = s.width
                    k0 = set_number("rwkv", s, j)
                    pe.wait_ge(S[f"w{k0 % 2}"], weights_in(k0))
                    for x in (1, 0, 2):
                        dense(pm[:, x, 0:w], lambda k: wts[:, k0 % 2, x, k, :], lambda k: hT[:, k, 0:w]).then_inc(S["raw_full"], 1)
                    c = slice(j * P, (j + 1) * P)
                    pe.matmul(pm[:, 3, 0:w], lora_wa[0:64, c], wl_al[0:64, 0:w], start=True, stop=True).then_inc(S["lo_full"], 1)
                    pe.matmul(pm[:, 4, 0:w], lora_wa[64:128, c], wl_al[64:128, 0:w], start=True, stop=True).then_inc(S["lo_full"], 1)
                    pe.matmul(pm[:, 5, 0:w], lora_g[:, c], gate_in[:, 0:w], start=True, stop=True).then_inc(S["lo_full"], 1)
                    tl.next(S["sq_ready"])
                    tl.next(S["raw_read"], 3)
                    pe.matmul(pm[:, 0, 0:w], ones2[:, :], sq[:, 0:w], start=True, stop=True).then_inc(S["n2_full"], 1)
                    tl.next(S["lo_sig"], 3)
                    tl.next(S["kr_ready"])
                    for c in range(s.chunks):
                        x = per_head(1, c * P, P, bt[:, cols(s, c)], kr[:, c].rearrange("p a t -> p (a t)"))
                    x.then_inc(S["g_full"], 1)
                    for c in range(s.chunks):
                        x = per_head(2, c * P, P, kt[:, cols(s, c)], kr[:, c].rearrange("p a t -> p (a t)"))
                    x.then_inc(S["g_full"], 1)
                    for c in range(s.chunks):
                        x = per_head(3, c * CH, CH, kr[:, c, 0, :], bt[:, cols(s, c)])
                    x.then_inc(S["g_full"], 1)
                    pe.matmul(pm[:, 4, 0:w], ones2[:, :], rkk[:, 0:w], start=True, stop=True).then_inc(S["bon_full"], 1)
                    for n, src in enumerate((kt, bt)):
                        for c in range(s.chunks):
                            for h in halves():
                                x = pe.matmul(pm[h, 5, n * SEG + c * CH:n * SEG + (c + 1) * CH], src[h, cols(s, c)], ident[h, h],
                                              start=True, stop=True, skip_group_check=True)
                    x.then_inc(S["tok_full"], 1)
                    tl.next(S["nrm_ready"])
                    for c in range(s.chunks):
                        for h in halves():
                            x = pe.matmul(pm[h, 0, cols(s, c)], rkv[h, 2, cols(s, c)], ident[h, h],
                                          start=True, stop=True, skip_group_check=True)
                    x.then_inc(S["tok_full"], 1)
                elif kind == "levels":
                    for l in range(1, 6):
                        tl.next(S["x_ready"])
                        tl.next(S["join_ready"])
                        for c in range(s.chunks):
                            x = per_head(1, c * CH, CH, joins[:, l - 1, c, :], xm[:, c, :])
                        x.then_inc(S["z_full"], 1)
                        tl.next(S["z_read"])
                        if l < 5:
                            for c in range(s.chunks):
                                per_head(2, c * CH, CH, xt[:, c, :], zs[:, c, :])
                        for c in range(s.chunks):
                            x = per_head(3, c * CH, CH, zs[:, c, :], xt[:, c, :])
                        x.then_inc(S["xz_full"], 1)
                elif kind == "chunks":
                    st = state[:, 1 if s.sample else 0, j, :]
                    tl.next(S["x_ready"])
                    tl.next(S["tok_read"], 2)
                    for c in range(s.chunks):
                        if c > 0:
                            tl.next(S["st_new"])
                        per_head(0, 0, HD, kr[:, c, 0, :], st, True, False)
                        per_head(0, 0, HD, mk_ak[:, c, 0, :], tok[:, 2, c, :], False, True).then_inc(S["p1_full"], 1)
                        per_head(5, c * CH, CH, st, kr[:, c, 1, :], True, False)
                        per_head(5, c * CH, CH, tok[:, 2, c, :], mk_ak[:, c, 1, :], False, False)
                        tl.next(S["p1_read"])
                        per_head(1, 0, HD, xt[:, c, :], p1s).then_inc(S["u_full"], 1)
                        per_head(2, 0, HD, tok[:, 0, c, :], tok[:, 2, c, :], True, False)
                        tl.next(S["u_read"])
                        per_head(2, 0, HD, tok[:, 1, c, :], us, False, True).then_inc(S["s_full"], 1)
                        x = per_head(5, c * CH, CH, us, lt_ab[:, c, 1, :], False, True)
                    x.then_inc(S["y_full"], 1)
                    tl.next(S["st_new"])
                    if s.last:
                        for h in halves():
                            x = pe.matmul(pm[h, 0, 0:HD], st[h], ident[h, h], start=True, stop=True)
                        x.then_inc(S["out_full"], 1)
                    w = s.width
                    tl.next(S["y_read"])
                    pe.matmul(pm[:, 3, 0:w], mean2[:, :], yraw[:, 0:w], start=True, stop=True).then_inc(S["mean_full"], 1)
                    tl.next(S["ysq_ready"])
                    pe.matmul(pm[:, 4, 0:w], mean2[:, :], sq[:, 0:w], start=True, stop=True).then_inc(S["var_full"], 1)
                    leave(pe, "pe")
                elif kind == "attn":
                    enter(pe, "pe", kind, s, j)
                    k0 = set_number("attn", s, j)
                    if s.past:
                        tl.next(S["hist"], 32)
                    if s.sample:
                        for b in range(4):
                            x = pe.transpose(pm[:, 4, b * P:(b + 1) * P], old_k[:, b, :], ident[:, :])
                        x.then_inc(S["old_full"], 1)
                    pe.wait_ge(S[f"w{k0 % 2}"], weights_in(k0))
                    for t in range(s.tiles):
                        dense(pm[0:s.rows, t, 0:3 * P].rearrange("p (x n) -> p x n", n=P), lambda k: hT[:, k, sl(s, t)],
                              lambda k: wts[:, k0 % 2, :, k, :]).then_inc(S["qkv_full"], 1)
                    for t in range(s.tiles):
                        tl.next(S["roped"])
                        for n in range(2):
                            x = pe.transpose(pm[:, 2 + t, n * P:n * P + s.rows], qk[0:s.rows, t, n * P:(n + 1) * P],
                                             ident[0:s.rows, 0:s.rows])
                        x.then_inc(S["qkT_full"], 1)
                    tl.next(S["qkT_read"], 2 * s.tiles)
                    if s.sample:
                        tl.next(S["old_read"])
                    for t in range(s.tiles):
                        r, nk = s.rows, s.past + t * P + s.rows
                        if t > 0:
                            tl.next(S["oT_read"])
                        for c in range(2):
                            hc = halves()[c]
                            for n in range(0, nk, 512):
                                m = min(512, nk - n)
                                x = pe.matmul(pm[0:r, 2 * c + n // 512, 0:m], qT[hc, sl(s, t)], keysT[hc, n:n + m], start=True, stop=True)
                        x.then_inc(S["sc_full"], 1)
                        tl.next(S["att_ready"])
                        nb = (nk + P - 1) // P
                        for b in range(nb):
                            m = min(P, nk - b * P)
                            x = pe.transpose(pm[0:m, 4 + b // 4, (b % 4) * P:(b % 4) * P + r], probs[0:r, 0, b * P:b * P + m], ident[0:r, 0:r])
                            if b % 4 == 3 or b == nb - 1:
                                x.then_inc(S["attT_full"], 1)
                        tl.next(S["attT_read"], (nb + 3) // 4)
                        for b in range(nb):
                            m = min(P, nk - b * P)
                            x = pe.matmul(pm[0:r, 0, 0:P], attT[0:m, b, 0:r], vals[0:m, b, :], start=(b == 0), stop=(b == nb - 1))
                        x.then_inc(S["o_full"], 1)
                        tl.next(S["o_ready"])
                        pe.transpose(pm[:, 1, 0:r], o_s[0:r], ident[0:r, 0:r]).then_inc(S["oT_full"], 1)
                    tl.next(S["oT_read"])
                    leave(pe, "pe")
                elif kind == "project":
                    enter(pe, "pe", kind, s, j)
                    for i in range(3):
                        k0 = set_number("out", s, i)
                        pe.wait_ge(S[f"w{k0 % 2}"], weights_in(k0))
                        for n in range(3 * i, min(3 * i + 3, KT)):
                            for t in range(s.tiles):
                                x = dense(pm[0:s.rows, 2 * t + n // 4, (n % 4) * P:(n % 4 + 1) * P], lambda k: mixT[:, k, sl(s, t)],
                                          lambda k: wts[:, k0 % 2, n % 3, k, :])
                        x.then_inc(S["wset"], 1)
                    for t in range(s.tiles):
                        tl.next(S["h_ready"])
                        transpose_tile(s, t, x1, 4)
                    tl.next(S["t_read"], 2)
                elif kind == "query":
                    for c in range(2 * PH):
                        k0 = set_number("q", s, c // 3)
                        if c % 3 == 0:
                            pe.wait_ge(S[f"w{k0 % 2}"], weights_in(k0))
                        dense(pm[:, c % 2, 0:s.width], lambda k: wts[:, k0 % 2, c % 3, k, :], lambda k: hT[:, k, 0:s.width]
                              ).then_inc(S["q_full"], 1)
                        tl.next(S["q_read"])
                        if c % 4 == 0 and c > 0:
                            tl.next(S["qs_read"])
                        for t in range(s.tiles):
                            x = pe.matmul(pm[0:s.rows, 2 + t, (c % 4) * NK:(c % 4 + 1) * NK], qsT[:, c % 2, sl(s, t)], skT[:, c, :],
                                          start=True, stop=True, skip_group_check=True)
                        x.then_inc(S["qs_full"], 1)
                    tl.next(S["qs_read"])
                    if s.last:
                        pe.transpose(pm[0:14, 4, 0:P], prev[:, 1 if s.sample else 0, :], ident[:, :]).then_inc(S["shift_full"], 1)
                elif kind == "topk":
                    if j == s.tiles - 1:
                        leave(pe, "pe")
                elif kind == "v":
                    g, (a, b) = s, j
                    seg, t = TILES[g]
                    if a == 0:
                        if g > 0:
                            pe.wait_ge(S["f_read"], g)
                        pe.wait_ge(S["weight_ready"], g + 1)
                        for c in range(2):
                            pe.matmul(pacc[0:seg.rows, c, :], zeros[0:seg.rows, 0:seg.rows], h1[0:seg.rows, g % 2, c * 512:(c + 1) * 512],
                                      start=True, stop=False, skip_group_check=True)
                    if b - a == 1:
                        sum_rows(g, seg, a)
                    else:
                        with pe.Fori(a, b) as i:
                            sum_rows(g, seg, i)
                elif kind == "finish":
                    seg, t = TILES[s]
                    for c in range(2):
                        x = pe.matmul(pacc[0:seg.rows, c, :], zeros[0:seg.rows, 0:seg.rows], h1[0:seg.rows, s % 2, c * 512:(c + 1) * 512],
                                      start=False, stop=True, skip_group_check=True)
                    x.then_inc(S["f_ready"], 1)

        @block.vector
        def _(v):
            tl = Tally(v, S["own_dve"])
            v.memset(dots8[:, :, :], 0.0).then_inc(S["peer_dve"], 1)
            v.wait_ge(S["peer_dve"], 1)
            v.nop().then_inc(S["peer_dve"], 1)
            v.nop().then_inc(S["peer_pe"], 1)
            v.nop().then_inc(S["peer_pe"], 1)
            v.nop().then_inc(S["dot_kept"], 1)
            v.nop().then_inc(S["dot_kept"], 1)
            v.wait_ge(S["consts"], 1)
            v.wait_ge(S["par_in"], 16 * 23)
            tl.link(v.tensor_tensor(eye2[:, :], ident[:, 0:HD], ident[:, HD:P], ALU.add))
            for i in range(2):
                x = v.tensor_tensor_reduce(lam_work[:, :], lam_in[:, 2 * i, :], lam_in[:, 2 * i + 1, :], 1.0, 0.0, ALU.mult, ALU.add,
                                           lam_sum[:, i:i + 1])
                if i == 0:
                    tl.link(x)
            tl.told(x, S["lam_ready"])
            v.wait_ge(S["lam_exp_ready"], 1)
            tl.link(v.tensor_tensor(neg_lam[:, :], lam_exp[:, 1:2], lam_exp[:, 0:1], ALU.subtract))
            tl.link(v.tensor_scalar(neg_lam[:, :], neg_lam[:, :], -LAM_INIT, None, ALU.add))
            tl.link(v.tensor_scalar(one_minus_ka[:, :], par[:, KAW:KAW + NJ], -1.0, 1.0, ALU.mult, ALU.add))
            tl.link(v.tensor_scalar(sub_scale[:, :], par[:, SUBG:SUBG + 1], 1.0 - LAM_INIT, None, ALU.mult))
            v.drain().then_inc(S["init_done"], 1)
            v.wait_ge(S["init_done"], 1)
            v.sem_inc(S["bar_dve"], 1)

            def layer_norm(x, stats, mv, sd, r, gain, said, dev, ready):
                for i in range(2):
                    tl.link(v.bn_stats(stats[0:r, i, :], x[:, i * 512:(i + 1) * 512]))
                tl.told(v.bn_aggr(mv[0:r], stats[0:r].rearrange("p a b -> p (a b)")), said)
                tl.next(dev)
                tl.link(v.reciprocal(sd[0:r], sd[0:r]))
                tl.link(v.tensor_scalar(x, x, mv[0:r, 0:1], sd[0:r], ALU.subtract, ALU.mult))
                tl.link(v.tensor_tensor(x, x, gain[0:r, 0, :], ALU.mult))
                tl.told(v.tensor_tensor(x, x, gain[0:r, 1, :], ALU.add), ready)

            def shift(dst, src, w, mu, kept, tmp):
                tl.link(v.tensor_copy(src[:, 0:1], kept))
                tl.link(v.tensor_tensor(tmp[:, 0:w], src[:, 0:w], src[:, 1:w + 1], ALU.subtract))
                tl.link(v.scalar_tensor_tensor(dst, tmp[:, 0:w], mu, src[:, 1:w + 1], ALU.mult, ALU.add))
                tl.link(v.tensor_copy(kept, src[:, w:w + 1]))

            def dot_rows(g, seg, i):
                r = slice(0, seg.rows)
                for half in range(2):
                    v.wait_ge(S["dot_kept"], i * 2 + half + 1 + 2 * ITERS * g)
                    for n in range(PIECE):
                        slot = half * PIECE + n
                        v.wait_ge(s_row[slot], i * 16 + 16 * (2 * ITERS * g + 1))
                        x = v.tensor_tensor_reduce(ring[r, slot, :], ring[r, slot, :], h1[r, g % 2, :], 1.0, 0.0, ALU.mult, ALU.add,
                                                   dots8[r, half, n:n + 1])
                    x.then_inc(S["peer_dve"], 1)
                    v.wait_ge(S["peer_dve"], i * 2 + half + 3 + 4 * ITERS * g)
                    v.tensor_copy(dots[r, bass.ds(i * RING + half * PIECE, PIECE)], dots8[r, half, :]).then_inc(S["dot_kept"], 1)

            def add_rows(g, seg, i):
                r = slice(0, seg.rows)
                m = PIECE - ON_PE
                for half in range(2):
                    for n in range(m):
                        slot = half * PIECE + ON_PE + n
                        v.wait_ge(s_row[slot], i * 16 + 16 * (2 * ITERS * g + ITERS + 1))
                        v.wait_ge(S["acc_made"], i * 2 * m + half * m + n + 1 + (2 * ITERS * m + 1) * g)
                        x = v.scalar_tensor_tensor(acc[r, :], ring[r, slot, :], wgt[r, bass.ds(i * RING + slot, 1)], acc[r, :],
                                                   ALU.mult, ALU.add)
                        x.then_inc(S["acc_made"], 1)
                    v.wait_ge(S["acc_made"], i * 2 * m + half * m + m + 1 + (2 * ITERS * m + 1) * g)
                    v.sem_inc(S["peer_dve"], 1)

            for kind, s, j in steps:
                if kind == "embed":
                    enter(v, "dve", kind, s, j)
                    tl.next(S["lnm_in"], 32)
                    for t in range(s.tiles):
                        tl.next(S[f"x_in{t}"], 16)
                        layer_norm(x_in[0:s.rows, t, :], st1, mv1, sd1, s.rows, ln_mix, S["mv"], S["sd"], S["h_ready"])
                    which = 1 if s.sample else 0
                    for x, dst in enumerate((wl_al, gate_in)):
                        tl.next(S["lora_read"])
                        shift(dst[:, 0:s.width], raw2[:, x, :], s.width, par[:, MU + 12 + x:MU + 13 + x], prev[:, which, 12 + x:13 + x], dif)
                    v.drain().then_inc(S["lora_mixed"], 1)
                    leave(v, "dve")
                elif kind == "rwkv":
                    enter(v, "dve", kind, s, j)
                    w = s.width
                    which = 1 if s.sample else 0
                    R, K, V = (rkv[:, x, 0:w] for x in range(3))

                    def chunked(x):
                        return x.rearrange("p (c t) -> p c t", t=CH)
                    for x in (1, 0, 2):
                        tl.next(S["raw_read"])
                        c = 4 * x + j
                        shift(rkv[:, x, 0:w], raw[:, x, :], w, par[:, MU + c:MU + c + 1], prev[:, which, c:c + 1], delta)
                        if x == 1:
                            tl.link(v.tensor_scalar(kk[:, 0:w], K, par[:, KKW + j:KKW + j + 1], None, ALU.mult))
                            tl.told(v.tensor_tensor(sq[:, 0:w], kk[:, 0:w], kk[:, 0:w], ALU.mult), S["sq_ready"])
                    tl.next(S["lo_sig"])
                    tl.link(v.tensor_scalar(lw[:, 0:w], lw[:, 0:w], DECAY, None, ALU.mult))
                    tl.link(v.tensor_tensor_scan(cum[:, 0:w], restart[:, 0:w], lw[:, 0:w], 0.0, ALU.mult, ALU.add))
                    tl.told(v.tensor_tensor(cumx[:, 0:w], cum[:, 0:w], lw[:, 0:w], ALU.subtract), S["cum_ready"])
                    tl.next(S["lo_sig"], 2)
                    tl.link(v.tensor_scalar(delta[:, 0:w], a_t[:, 0:w], par[:, KAW + j:KAW + j + 1], one_minus_ka[:, j:j + 1], ALU.mult, ALU.add))
                    tl.link(v.tensor_tensor(K, K, delta[:, 0:w], ALU.mult))
                    tl.link(v.scalar_tensor_tensor(rkk[:, 0:w], K, par[:, RKW + j:RKW + j + 1], R, ALU.mult, ALU.mult))
                    tl.next(S["nrm_ready"])
                    tl.link(v.tensor_scalar(nrm[:, 0:w], nrm[:, 0:w], 1e-12, None, ALU.max))
                    tl.link(v.reciprocal(nrm[:, 0:w], nrm[:, 0:w]))
                    tl.link(v.tensor_tensor(kk[:, 0:w], kk[:, 0:w], nrm[:, 0:w], ALU.mult))
                    tl.link(v.scalar_tensor_tensor(sq[:, 0:w], kk[:, 0:w], -1.0, a_t[:, 0:w], ALU.mult, ALU.mult))
                    tl.next(S["exps"])
                    tl.link(v.tensor_tensor(kr[:, 0:s.chunks, 0, :], chunked(kk[:, 0:w]), chunked(dec_x[:, 0:w]), ALU.mult))
                    tl.link(v.tensor_tensor(kr[:, 0:s.chunks, 1, :], chunked(R), chunked(dec_i[:, 0:w]), ALU.mult))
                    tl.link(v.tensor_tensor(kt[:, 0:w], K, dec_n[:, 0:w], ALU.mult))
                    tl.told(v.tensor_tensor(bt[:, 0:w], sq[:, 0:w], dec_n[:, 0:w], ALU.mult), S["kr_ready"])
                    n = s.chunks

                    def gram(bank, width):
                        return pm[:, bank, 0:n * width].rearrange("p (c t) -> p c t", t=width)
                    mask = causal[:, :, :].rearrange("p a t -> p (a t)")[:, None, :].to_broadcast([P, n, P])
                    tl.next(S["g_full"])
                    tl.told(v.tensor_tensor(lt_ab[:, 0:n].rearrange("p c a t -> p c (a t)"), gram(1, P), mask, ALU.mult), S["masked"])
                    tl.next(S["g_full"])
                    tl.link(v.tensor_tensor(mk_ak[:, 0:n].rearrange("p c a t -> p c (a t)"), gram(2, P), mask, ALU.mult))
                    tl.next(S["g_full"])
                    eye = eye2[:, None, :].to_broadcast([P, n, CH])
                    tl.link(v.tensor_tensor(xm[:, 0:n, :], gram(3, CH), first_lo[:, None, :].to_broadcast([P, n, CH]), ALU.mult))
                    tl.link(v.tensor_tensor(xm[:, 0:n, :], xm[:, 0:n, :], eye, ALU.add))
                    tl.link(v.tensor_tensor(xt[:, 0:n, :], lt_ab[:, 0:n, 0, :], lower[:, 0, None, :].to_broadcast([P, n, CH]), ALU.mult))
                    tl.told(v.tensor_tensor(xt[:, 0:n, :], xt[:, 0:n, :], eye, ALU.add), S["x_ready"])
                    tl.next(S["bon_full"])
                    tl.link(v.tensor_tensor(bonus[:, 0:w], pm[:, 4, 0:w], V, ALU.mult))
                elif kind == "levels":
                    n = s.chunks
                    for l in range(1, 6):
                        tl.next(S["xz_full"])
                        if l < 5:
                            tl.link(v.tensor_tensor(xm[:, 0:n, :], pm[:, 2, 0:s.width].rearrange("p (c t) -> p c t", t=CH), xm[:, 0:n, :], ALU.add))
                        tl.told(v.tensor_tensor(xt[:, 0:n, :], pm[:, 3, 0:s.width].rearrange("p (c t) -> p c t", t=CH), xt[:, 0:n, :], ALU.add),
                                S["x_ready"])
                elif kind == "chunks":
                    w = s.width
                    st = state[:, 1 if s.sample else 0, j, :]
                    for c in range(s.chunks):
                        last = dec_i[:, c * CH + CH - 1:c * CH + CH]
                        tl.link(v.tensor_scalar(s_dec, st, last, None, ALU.mult))
                        tl.next(S["p1_full"])
                        tl.told(v.tensor_copy(p1s, pm[:, 0, 0:HD]), S["p1_read"])
                        tl.next(S["u_full"])
                        tl.told(v.tensor_copy(us, pm[:, 1, 0:HD]), S["u_read"])
                        tl.next(S["s_full"])
                        tl.told(v.scalar_tensor_tensor(st, pm[:, 2, 0:HD], last, s_dec, ALU.mult, ALU.add), S["st_new"])
                    tl.next(S["mean_full"])
                    tl.link(v.tensor_tensor(yraw[:, 0:w], yraw[:, 0:w], pm[:, 3, 0:w], ALU.subtract))
                    tl.told(v.tensor_tensor(sq[:, 0:w], yraw[:, 0:w], yraw[:, 0:w], ALU.mult), S["ysq_ready"])
                    tl.next(S["ysd"])
                    tl.link(v.reciprocal(nrm[:, 0:w], nrm[:, 0:w]))
                    tl.link(v.tensor_tensor(yraw[:, 0:w], yraw[:, 0:w], nrm[:, 0:w], ALU.mult))
                    tl.link(v.tensor_scalar(yraw[:, 0:w], yraw[:, 0:w], par[:, LXG + j:LXG + j + 1], par[:, LXB + j:LXB + j + 1], ALU.mult, ALU.add))
                    tl.link(v.tensor_tensor(yraw[:, 0:w], yraw[:, 0:w], bonus[:, 0:w], ALU.add))
                    tl.link(v.tensor_tensor(mixT[:, j, 0:w], yraw[:, 0:w], g_t[:, 0:w], ALU.mult))
                    leave(v, "dve")
                elif kind == "attn":
                    enter(v, "dve", kind, s, j)
                    for t in range(s.tiles):
                        tl.next(S["qkv_read"])
                        r = s.rows
                        x = qk[0:r, t, :].rearrange("p (g d) -> p g d", d=HD)
                        xa, xb = x[:, :, 0:8], x[:, :, 8:16]
                        g = s.first_tile + t
                        cos = rope[0:r, g, None, 0:8].to_broadcast([r, 4, 8])
                        sin = rope[0:r, g, None, 8:16].to_broadcast([r, 4, 8])
                        tl.link(v.tensor_tensor(r1[0:r], xa, cos, ALU.mult))
                        tl.link(v.tensor_tensor(r2[0:r], xb, sin, ALU.mult))
                        tl.link(v.tensor_tensor(r3[0:r], xb, cos, ALU.mult))
                        tl.link(v.tensor_tensor(r4[0:r], xa, sin, ALU.mult))
                        tl.link(v.tensor_tensor(xa, r1[0:r], r2[0:r], ALU.subtract))
                        tl.told(v.tensor_tensor(xb, r3[0:r], r4[0:r], ALU.add), S["roped"])
                    for t in range(s.tiles):
                        r, nk = s.rows, s.past + t * P + s.rows
                        tl.next(S["sc_full"])
                        sc2 = pm[0:r, 0:4, :].rearrange("p (c a) n -> p c (a n)", c=2)
                        if not s.sample:
                            tl.link(v.memset(sc2[0:CH, :, nk - CH:nk], -1.0e30))
                        tl.link(v.tensor_reduce(mx[0:r], sc2[:, :, 0:nk], AX.X, ALU.max))
                        tl.told(v.tensor_scalar(negm[0:r], mx[0:r], -DA_SCALE, None, ALU.mult), S["max_ready"])
                        tl.next(S["prob_ready"])
                        tl.link(v.reciprocal(rz[0:r], zsum[0:r]))
                        tl.link(v.tensor_scalar(ratio[0:r], zsum[0:r, 0:1], rz[0:r, 1:2], neg_lam[0:r, :], ALU.mult, ALU.mult))
                        tl.told(v.scalar_tensor_tensor(probs[0:r, 0, 0:nk], probs[0:r, 1, 0:nk], ratio[0:r], probs[0:r, 0, 0:nk],
                                                       ALU.mult, ALU.add), S["att_ready"])
                        tl.next(S["rms_ready"])
                        tl.link(v.reciprocal(rms[0:r], rms[0:r]))
                        tl.told(v.tensor_scalar(o_s[0:r], o_s[0:r], rms[0:r], None, ALU.mult), S["o_ready"])
                    leave(v, "dve")
                elif kind == "project":
                    enter(v, "dve", kind, s, j)
                    tl.next(S["lnm_in"], 32)
                    tl.next(S["res_in"], 16 * s.tiles)
                    tl.next(S["wset"], 3)
                    for t in range(s.tiles):
                        x = x1[0:s.rows, t, :]
                        tl.link(v.scalar_tensor_tensor(x, x, ALPHA, pm[0:s.rows, 2 * t:2 * t + 2, :].rearrange("p a n -> p (a n)"),
                                                       ALU.mult, ALU.add))
                        layer_norm(x, st3, mv3, sd3, s.rows, ln_mix, S["mv"], S["sd"], S["h_ready"])
                elif kind == "topk":
                    r, t = s.rows, j
                    if t == 0:
                        tl.next(S["qs_read"], 4)
                        v.wait_ge(S["h1_stored"], 16 * (s.first_tile + s.tiles))
                    for c in range(2 * PH):
                        x = scores[0:r, t, c, :]
                        top16(v, tl, x, work[0:r, :], v16[0:r, c, :], i16[0:r, c, :])
                    tl.link(v.tensor_copy(i16f[0:r], i16[0:r]))
                    one = v16[0:r].rearrange("p (h c) k -> p h c k", c=2)
                    s1, s2 = one[:, :, 0, :], one[:, :, 1, :]
                    left = cand[0:r, :, 0:ROW_A * TOPK].rearrange("p h (a b) -> p h a b", a=ROW_A)
                    rest = cand[0:r, :, ROW_A * TOPK:NCAND].rearrange("p h (a b) -> p h a b", a=ROW_B)
                    tl.link(v.tensor_tensor(left, s1[:, :, 0:ROW_A, None].to_broadcast([r, PH, ROW_A, TOPK]),
                                            s2[:, :, None, :].to_broadcast([r, PH, ROW_A, TOPK]), ALU.add))
                    tl.link(v.tensor_tensor(rest, s1[:, :, ROW_A:TOPK, None].to_broadcast([r, PH, ROW_B, 4]),
                                            s2[:, :, None, 0:4].to_broadcast([r, PH, ROW_B, 4]), ALU.add))
                    for h in range(PH):
                        top16(v, tl, cand[0:r, h, :], work[0:r, 0:NCAND], t16[0:r, h, :], pos[0:r, h, :])
                    tl.link(v.tensor_copy(hmax[0:r], t16[0:r, :, 0]))
                    tl.told(v.tensor_tensor(t16[0:r], t16[0:r], hmax[0:r, :, None].to_broadcast([r, PH, TOPK]), ALU.subtract), S["max_exp"])
                    p_flat = pos[0:r].rearrange("p h k -> p (h k)")
                    tl.link(v.tensor_scalar(posb[0:r, 0], p_flat, 4, None, ALU.logical_shift_right))
                    tl.link(v.tensor_scalar(posb[0:r, 1], p_flat, 15, None, ALU.bitwise_and))
                    tl.link(v.tensor_scalar(posb[0:r, 2], p_flat, 2, None, ALU.logical_shift_right))
                    tl.link(v.tensor_scalar(posb[0:r, 3], p_flat, 3, None, ALU.bitwise_and))

                    def flat(x):
                        return x[0:r].rearrange("p h k -> p (h k)")
                    tl.link(v.tensor_scalar(flat(pos_f), p_flat, float(ROW_A * TOPK), None, ALU.is_ge))
                    for out, lo, hi, off in ((af, 0, 2, -12.0), (bf, 1, 3, 0.0)):
                        tl.link(v.tensor_copy(flat(out), posb[0:r, lo]))
                        tl.link(v.scalar_tensor_tensor(flat(e1), posb[0:r, hi], off, flat(out), ALU.add, ALU.subtract))
                        tl.link(v.tensor_tensor(flat(e1), flat(e1), flat(pos_f), ALU.mult))
                        tl.link(v.tensor_tensor(flat(out), flat(out), flat(e1), ALU.add))
                    keys = i16f[0:r].rearrange("p (h c) k -> p h c k", c=2)
                    for c, (rank, out) in enumerate(((af, e1), (bf, e2))):
                        tl.link(v.tensor_tensor(hot[0:r], flat(rank)[:, :, None].to_broadcast([r, SLOTS, TOPK]),
                                                iota16[0:r, None, :].to_broadcast([r, SLOTS, TOPK]), ALU.is_equal))
                        hot4 = hot[0:r].rearrange("p (h e) k -> p h e k", h=PH)
                        tl.link(v.tensor_tensor(hot4, hot4, keys[:, :, c, None, :].to_broadcast([r, PH, TOPK, TOPK]), ALU.mult))
                        tl.link(v.tensor_reduce(flat(out), hot[0:r], AX.X, ALU.add))
                    tl.link(v.scalar_tensor_tensor(idx[0:r, s.n % 2, t, :], flat(e1), float(NK), flat(e2), ALU.mult, ALU.add))
                    tl.next(S["exp_ready"])
                    tl.link(v.tensor_reduce(hmax[0:r], t16[0:r], AX.X, ALU.add))
                    tl.link(v.reciprocal(hmax[0:r], hmax[0:r]))
                    tl.told(v.tensor_tensor(gates[0:r, s.n % 2, t, :].rearrange("p (h k) -> p h k", h=PH), t16[0:r],
                                            hmax[0:r, :, None].to_broadcast([r, PH, TOPK]), ALU.mult), S["idx_ready"])
                    if t == s.tiles - 1:
                        leave(v, "dve")
                elif kind == "u":
                    g, (a, b) = s, j
                    seg, t = TILES[g]
                    if a == 0:
                        tl.next(S[f"h1_in{g % 2}"], 16)
                        if g > 0:
                            v.wait_ge(S["weight_ready"], g)
                    if b - a == 1:
                        dot_rows(g, seg, a)
                    else:
                        with v.Fori(a, b) as i:
                            dot_rows(g, seg, i)
                elif kind == "gate":
                    seg, t = TILES[s]
                    r = slice(0, seg.rows)
                    if s > 0:
                        v.wait_ge(S["peer_pe"], 2 * ITERS * s + 2)
                    tl.next(S["gelu_done"])
                    v.tensor_tensor(wgt[r, :], dots[r, :], gates[r, seg.n % 2, t, :], ALU.mult).then_inc(S["weight_ready"], 1)
                    v.wait_ge(S["weight_ready"], s + 1)
                    v.memset(acc[r, :], 0.0).then_inc(S["acc_made"], 1)
                elif kind == "v":
                    g, (a, b) = s, j
                    seg, t = TILES[g]
                    if b - a == 1:
                        add_rows(g, seg, a)
                    else:
                        with v.Fori(a, b) as i:
                            add_rows(g, seg, i)
                elif kind == "finish":
                    seg, t = TILES[s]
                    r = slice(0, seg.rows)
                    x = h1[r, s % 2, :]
                    tl.next(S["f_ready"])
                    tl.link(v.scalar_tensor_tensor(x, x, ALPHA, acc[r, :], ALU.mult, ALU.add))
                    tl.told(v.tensor_tensor(x, x, pacc[r, :, :].rearrange("p a n -> p (a n)"), ALU.add), S["f_read"])
                    layer_norm(x, st2, mv2, sd2, seg.rows, ln2, S["mv2s"], S["sd2s"], S["y_ready"])


def top16(v, tl, x, work, values, places):
    tl.link(v.max(values[:, 0:8], x))
    tl.link(v.max_index(places[:, 0:8], values[:, 0:8], x))
    tl.link(v.match_replace(work, values[:, 0:8], x, LOW))
    tl.link(v.max(values[:, 8:16], work))
    tl.link(v.max_index(places[:, 8:16], values[:, 8:16], work))


_INS = ['x_prompt', 'x_sample', 'cache_k', 'cache_v', 'state_wkv', 'state_shift', 'ln_in_g', 'ln_in_b',
        'w_in', 'shift_mu', 'rw_w0', 'rw_w2', 'rw_a0', 'rw_a2', 'rw_g2', 'rw_kk', 'rw_ka', 'rw_rk', 'rw_lnx_g',
        'rw_lnx_b', 'da_lq1', 'da_lk1', 'da_lq2', 'da_lk2', 'da_subln_g', 'w_out', 'ln1_g', 'ln1_b',
        'peer_wq', 'peer_subkeys', 'peer_u', 'peer_v', 'ln2_g', 'ln2_b']
_OUTS = [(1, 1024, 1024), (1, 64, 1024), (1, 1, 1024, 4, 128), (1, 1, 1024, 4, 128), (1, 1, 8, 64, 64),
         (1, 1, 1, 1792), (1, 1, 64, 4, 128), (1, 1, 64, 4, 128), (1, 1, 8, 64, 64), (1, 1, 1, 1792)]


def rope_tables():
    half = ROT // 2
    pos = np.concatenate([np.arange(SEQ), PAST + np.arange(DEC)]).astype(np.float32)
    inv = np.power(np.float32(THETA), -np.arange(half, dtype=np.float32) * np.float32(2.0 / ROT)).astype(np.float32)
    ang = pos[:, None] * inv[None, :]
    return np.concatenate([np.cos(ang), np.sin(ang)], 1).astype(np.float32)


def kernel(**inputs):
    import concourse.bacc as bacc
    from concourse.bass_utils import run_bass_kernel_spmd as run

    nc = bacc.Bacc("TRN2", target_bir_lowering=False, num_devices=1)
    arrays, ins = {}, {}
    for name in _INS:
        arrays[f"in_{name}"] = np.ascontiguousarray(inputs[name])
        ins[name] = nc.dram_tensor(f"in_{name}", arrays[f"in_{name}"].shape, F32, kind="ExternalInput").ap()
    arrays["in_rope"] = rope_tables()
    ins["rope"] = nc.dram_tensor("in_rope", arrays["in_rope"].shape, F32, kind="ExternalInput").ap()
    outs = [nc.dram_tensor(f"out_{i}", shape, F32, kind="ExternalOutput").ap() for i, shape in enumerate(_OUTS)]
    build(nc, ins, outs)
    r = run(nc, [arrays], core_ids=[0])
    return tuple(r.results[0][f"out_{i}"] for i in range(len(_OUTS)))
```

```python
from contextlib import ExitStack
import math

import numpy as np
import concourse.bass as bass
from concourse import mybir

F32 = mybir.dt.float32
I32 = mybir.dt.int32
U32 = mybir.dt.uint32
ALU = mybir.AluOpType
ACT = mybir.ActivationFunctionType
AX = mybir.AxisListType

P = 128
D = 1024
KT = D // P
SEQ, DEC, PAST = 1024, 64, 512
CH = 64
HD = 64
RW = 512
NJ = RW // P
RW_COLS = 1792
DA = 512
ROT = 16
THETA = 500000.0
DA_SCALE = HD ** -0.5
LAM_INIT = 0.8 - 0.6 * math.exp(-0.3 * 0)
ALPHA = 2.0 ** 0.25
LN_EPS, GN_EPS = 1e-5, 64e-5
DECAY = -math.exp(-0.5)
PH, NK, TOPK = 8, 128, 16
SLOTS = PH * TOPK
SEG = 256
NCH = SEG // CH
NT = SEG // P
PIECE = 4
RING = 4 * PIECE
ON_PE = 3
ON_PE_LAST = 1
ITERS = SLOTS // (2 * PIECE)
PIECES = SLOTS // PIECE
MU, W0, A0, KKW, KAW, RKW, LXG, LXB, SHIFT, SUBG = 0, 14, 18, 22, 26, 30, 34, 38, 42, 56
NPAR = 57
ROW_A, ROW_B = 4, 12
NCAND = ROW_A * TOPK + ROW_B * 4
LOW = -3.0e38


class Segment:
    def __init__(self, n, sample, start, width):
        self.n, self.sample, self.start, self.width = n, sample, start, width
        self.rows = min(width, P)
        self.tiles = (width + P - 1) // P
        self.chunks = width // CH
        self.last = sample or start + width == SEQ
        self.past = PAST if sample else start
        self.first_tile = n * NT
        self.pos = (SEQ if sample else start)


SEGMENTS = [Segment(i, False, i * SEG, SEG) for i in range(SEQ // SEG)] + [Segment(SEQ // SEG, True, 0, DEC)]
TILES = [(s, t) for s in SEGMENTS for t in range(s.tiles)]


def mix_steps(s):
    steps = [("embed", s, 0)]
    for j in range(NJ):
        steps += [("rwkv", s, j), ("levels", s, j), ("chunks", s, j), ("attn", s, j)]
    steps += [("project", s, 0), ("query", s, 0)]
    steps += [("topk", s, t) for t in range(s.tiles)]
    return steps


def on_pe(g):
    return ON_PE_LAST if g == len(TILES) - 1 else ON_PE


MIX_STEPS = [x for s in SEGMENTS for x in mix_steps(s)]


def cuts(kind, s):
    if kind == "embed":
        return [("tile", 1, 5)] * s.tiles + [("lora", 9, 0), ("end", 0.5, 5)]
    if kind == "rwkv":
        return [("raw", 9, 0), ("shifted", 0.5, 5), ("decay", 1, 9), ("grams", 5, 3)]
    if kind == "levels":
        return [("level", 3.7, 0.7)] * 5
    if kind == "chunks":
        return [("p1", 1, 0.6), ("u", 1, 0.6), ("state", 1, 0.6)] * s.chunks + [("mean", 1.5, 1), ("variance", 1.5, 1), ("end", 0.5, 5)]
    if kind == "attn":
        return ([("qkv", 8, 0), ("rope", 1.5, 3)] + [("scores", 1.5, 0), ("max", 2.5, 3), ("probs", 4, 1), ("out", 1, 1.5)] * s.tiles
                + [("end", 0.5, 0.5)])
    if kind == "project":
        return [("set", 10, 0)] * 3 + [("tile", 1, 6)] * s.tiles
    if kind == "query":
        return [("query", 4.3, 0.3)] * (2 * PH)
    return [("keys", 0.1, 1.9)] * (2 * PH) + [("pairs", 0.1, 1.9)] * PH + [("ranks", 0.5, 4), ("first", 0.5, 7), ("second", 0.5, 9)]


def spread(g, mixes):
    parts = [(q, part) for q in range(PIECES) for part in range(2)]
    left_u, left_v = list(parts), list(parts) if g > 0 else []
    order = [("open", g, None)]
    all_u, all_v = sum(x[1] for x in mixes), sum(x[2] for x in mixes)
    sum_u = sum_v = 0.0
    for name, free_u, free_v in mixes:
        order.append(("mix", None, name))
        sum_u, sum_v = sum_u + free_u / all_u, sum_v + free_v / all_v
        while True:
            due_u = bool(left_u) and len(parts) - len(left_u) < round(sum_u * len(parts))
            due_v = bool(left_v) and len(parts) - len(left_v) < round(sum_v * len(parts))
            if due_u:
                order.append(("u", g, left_u.pop(0)))
            if due_v:
                order.append(("v", g - 1, left_v.pop(0)))
            if not due_u and not due_v:
                break
    assert not left_u and not left_v
    return order + [("close", g, None)]


def plan():
    order = [("mix", None, x[0]) for st in mix_steps(SEGMENTS[0]) for x in cuts(st[0], st[1])]
    for s in SEGMENTS[:-1]:
        mixes = [x for st in mix_steps(SEGMENTS[s.n + 1]) for x in cuts(st[0], st[1])]
        rounds = range(s.first_tile, s.first_tile + s.tiles)
        share, at, half = [x[1] / sum(y[1] for y in mixes) + x[2] / sum(y[2] for y in mixes) for x in mixes], 0, 0.0
        for g in rounds:
            end = at
            while end < len(mixes) and (g == rounds[-1] or half < 2.0 * (g - rounds[0] + 1) / s.tiles):
                half += share[end]
                end += 1
            order += spread(g, mixes[at:end])
            at = end
    for g in range(SEGMENTS[-1].first_tile, len(TILES) + 1):
        order += [("open", g, None), ("turns", g, None), ("close", g, None)]
    return order


class Tally:

    def __init__(self, eng, own):
        self.eng, self.own, self.seen, self.made = eng, own, {}, 0

    def next(self, sem, n=1):
        self.seen[sem.name] = self.seen.get(sem.name, 0) + n
        self.eng.wait_ge(sem, self.seen[sem.name])

    def rounds(self, sem, n=1):
        if self.seen.get(sem.name, 0):
            self.eng.wait_ge(sem, self.seen[sem.name])
        self.seen[sem.name] = self.seen.get(sem.name, 0) + n

    def link(self, ins):
        self.made += 1
        ins.then_inc(self.own, 1)
        self.eng.wait_ge(self.own, self.made)

    def told(self, ins, sem):
        ins.then_inc(sem, 1)
        self.next(sem)


def build(nc, ins, outs):
    (y_p, y_s, k_p, v_p, wkv_p, sh_p, k_s, v_s, wkv_s, sh_s) = outs
    order = plan()
    ctx = ExitStack()
    with ctx:
        def sb(name, shape, dt=F32):
            return ctx.enter_context(nc.sbuf_tensor(name, shape, dt))

        def sem(name):
            return ctx.enter_context(nc.semaphore(name))

        h_d = nc.dram_tensor("h_scratch", (SEG, D), F32, kind="Internal").ap()
        h1_d = nc.dram_tensor("h1_scratch", (len(TILES) * P, D), F32, kind="Internal").ap()
        kt_d = nc.dram_tensor("keys_scratch", (NJ, P, SEQ), F32, kind="Internal").ap()

        ident = sb("ident", [P, P])
        eye2 = sb("eye2", [P, HD])
        ones2 = sb("ones2", [P, P])
        mean2 = sb("mean2", [P, P])
        causal = sb("causal", [P, 2, CH])
        first_lo = sb("first_lo", [P, CH])
        lower = sb("lower", [P, 6, CH])
        restart = sb("restart", [P, SEG])
        iota16 = sb("iota16", [P, TOPK])
        zeros = sb("zeros", [P, P])
        eps_ln = sb("eps_ln", [P, 1])
        eps_gn = sb("eps_gn", [P, 1])
        par = sb("par", [P, NPAR])
        one_minus_ka = sb("one_minus_ka", [P, NJ])
        sub_scale = sb("sub_scale", [P, 1])
        neg_lam = sb("neg_lam", [P, 1])
        shift_rows = sb("shift_rows", [14, P])
        lam_sum = sb("lam_sum", [P, 2])
        lam_exp = sb("lam_exp", [P, 2])
        lora_wa = sb("lora_wa", [P, RW])
        lora_g = sb("lora_g", [P, RW])
        rope = sb("rope", [P, len(TILES), ROT])
        skT = sb("skT", [P, 2 * PH, NK])
        ln2 = sb("ln2", [P, 2, D])

        hT = sb("hT", [P, KT, SEG])
        mixT = sb("mixT", [P, KT, SEG])
        wts = sb("wts", [P, 2, 3, KT, P])
        wl_al = sb("wl_al", [P, SEG])
        gate_in = sb("gate_in", [P, SEG])
        prev = sb("prev", [P, 2, 14])
        state = sb("state", [P, 2, NJ, HD])
        idx = sb("idx", [P, 2, NT, SLOTS], I32)
        gates = sb("gates", [P, 2, NT, SLOTS])

        ring = sb("ring", [P, RING, D])
        stage = sb("stage", [P, 2, 2, PIECE], I32)
        h1 = sb("h1", [P, 3, D])
        dots8 = sb("dots8", [P, 2, PIECE])
        dots = sb("dots", [P, SLOTS])
        wgt = sb("wgt", [P, SLOTS])
        diag = sb("diag", [P, 2, ON_PE, P])
        acc = sb("acc", [P, D])
        st2 = sb("st2", [P, 2, 6])
        mv2 = sb("mv2", [P, 2])
        sd2 = sb("sd2", [P, 1])

        ARENA = 10560
        arena = sb("arena", [P, ARENA])
        top = [0]

        def carve(*shape):
            n = int(np.prod(shape))
            a = arena[:, top[0]:top[0] + n]
            top[0] += n
            assert top[0] <= ARENA, top[0]
            if len(shape) == 1:
                return a
            names = "abcd"[:len(shape)]
            kw = {c: v for c, v in zip(names[1:], shape[1:])}
            return a.rearrange(f"p ({' '.join(names)}) -> p {' '.join(names)}", **kw)

        top[0] = 3000
        ln_mix = carve(2, D)
        top[0] = 0
        x_in = carve(NT, D)
        st1 = carve(2, 6)
        mv1 = carve(2)
        sd1 = carve(1)
        raw2 = carve(2, SEG + 1)
        dif = carve(SEG)
        assert top[0] <= 3000
        top[0] = 0
        raw = carve(3, SEG + 1)
        rkv = carve(3, SEG)
        delta = carve(SEG)
        lw = carve(SEG)
        cum = carve(SEG)
        cumx = carve(SEG)
        a_t = carve(SEG)
        g_t = carve(SEG)
        dec_i = carve(SEG)
        dec_x = carve(SEG)
        dec_n = carve(SEG)
        kk = carve(SEG)
        sq = carve(SEG)
        nrm = carve(SEG)
        rkk = carve(SEG)
        kr = carve(NCH, 2, CH)
        kt = carve(SEG)
        bt = carve(SEG)
        bonus = carve(SEG)
        lt_ab = carve(NCH, 2, CH)
        mk_ak = carve(NCH, 2, CH)
        xm = carve(NCH, CH)
        xt = carve(NCH, CH)
        zs = carve(NCH, CH)
        joins = carve(5, NCH, CH)
        tok = carve(3, NCH, CH)
        p1s = carve(HD)
        us = carve(HD)
        s_dec = carve(HD)
        yraw = carve(SEG)
        s_out = carve(HD)
        top[0] = 0
        keysT = carve(SEQ)
        vals = carve(KT, P)
        qT = carve(SEG)
        qk = carve(NT, 2 * P)
        old_k = carve(4, P)
        r1 = carve(4, 8)
        r2 = carve(4, 8)
        r3 = carve(4, 8)
        r4 = carve(4, 8)
        probs = carve(2, SEQ)
        attT = carve(KT, P)
        mx = carve(2)
        negm = carve(2)
        zsum = carve(2)
        rz = carve(2)
        ratio = carve(1)
        o_s = carve(P)
        o_sq = carve(P)
        ss = carve(1)
        rms = carve(1)
        top[0] = 0
        x1 = carve(NT, D)
        st3 = carve(2, 6)
        mv3 = carve(2)
        sd3 = carve(1)
        qsT = carve(2, SEG)
        top[0] = 3000
        scores = carve(NT, 2 * PH, NK)
        v16 = carve(2 * PH, TOPK)
        i16f = carve(2 * PH, TOPK)
        work = carve(NK)
        t16 = carve(PH, TOPK)
        pos_f = carve(PH, TOPK)
        af = carve(PH, TOPK)
        bf = carve(PH, TOPK)
        e1 = carve(PH, TOPK)
        e2 = carve(PH, TOPK)
        hmax = carve(PH)
        top[0] = 0
        cand = carve(PH, NCAND)
        hot = carve(SLOTS, TOPK)
        top[0] = 8600
        i16 = carve(2 * PH, TOPK).bitcast(U32)
        pos = carve(PH, TOPK).bitcast(U32)
        posb = carve(4, PH * TOPK).bitcast(U32)
        top[0] = 9600
        lam_in = carve(4, HD)
        lam_work = carve(HD)

        pm = ctx.enter_context(nc.psum_tensor("pm", [P, 6, 512], F32))
        pacc = ctx.enter_context(nc.psum_tensor("pacc", [P, 2, 512], F32))

        names = """own_dve own_act own_pool own_pe bar_sp bar_act bar_pe bar_dve par_in par_full consts
            sub_full sub_read lam_ready lam_exp_ready x_in0 x_in1 w0 w1 h_stored mv sd h_ready t_full t_read
            lora_full lora_read lora_mixed raw_full raw_read lo_full lo_sig cum_ready exps sq_ready n2_full
            nrm_ready kr_ready g_full masked bon_full tok_full tok_read join_ready x_ready z_full z_read
            xz_full x_new p1_full p1_read u_full u_read s_full st_new y_full y_read mean_full ysq_ready var_full
            ysd out_full out_read st_stored hist old_full old_read qkv_full qkv_read roped kv_stored qkT_full
            qkT_read kt_stored sc_full max_ready prob_ready att_ready attT_full attT_read o_full o_read o_ready
            oT_full oT_read rms_ready res_in wset m_read q_full q_read qs_full qs_read h1_stored idx_ready
            shift_full shift_read shift_stored staged_u staged_v parked parked_pe u_used v_added v_summed dot_kept gelu_done
            weight_ready diag_ready acc_made f_ready f_read mv2s sd2s y_ready y_stored h1_in0 h1_in1 h1_in2 lnm_in
            max_exp exp_ready rwkv_init init_done topk_done""".split()
        S = {n: sem(n) for n in names}
        s_row = [sem(f"row{r}") for r in range(RING)]

        block = ctx.enter_context(nc.Block())

        PHASE_OF = {}
        for st in MIX_STEPS:
            if st[0] in ("embed", "rwkv", "attn", "project"):
                PHASE_OF[(st[0], st[1].n, st[2])] = len(PHASE_OF)
        PHASE_LIST = sorted(PHASE_OF, key=PHASE_OF.get)

        def enter(eng, me, kind, s, j):
            n = PHASE_OF[(kind, s.n, j)] + 1
            for other in ("sp", "act", "pe", "dve"):
                if other != me:
                    eng.wait_ge(S["bar_" + other], n)

        def leave(eng, me):
            eng.drain().then_inc(S["bar_" + me], 1)

        def u_slot(half, n):
            return half * 2 * PIECE + n

        def v_slot(half, n):
            return half * 2 * PIECE + PIECE + n

        def turns(eng, g, units):
            with eng.Fori(0, ITERS) as i:
                for half in range(2):
                    units(g, i, half)

        def interleave(mixing, u_part, v_part, units, extra, eng):
            for kind, g, arg in order:
                if kind == "mix":
                    assert next(mixing) == arg
                elif kind == "u":
                    u_part(g, arg[0] // 2, arg[0] % 2, arg[1])
                elif kind == "v":
                    v_part(g, arg[0] // 2, arg[0] % 2, arg[1])
                elif kind == "turns":
                    turns(eng, g, units)
                else:
                    extra(kind, g)
            assert next(mixing, None) is None

        def sl(s, t):
            return slice(t * P, t * P + s.rows)

        def cols(s, c):
            return slice(c * CH, c * CH + CH)

        def halves():
            return (slice(0, HD), slice(HD, P))

        def x_rows(s, t):
            src = ins["x_sample"] if s.sample else ins["x_prompt"]
            return src[0, s.start + t * P:s.start + t * P + s.rows, :]

        w_in = ins["w_in"][0].rearrange("(k p) n -> p k n", p=P)
        w_out = ins["w_out"][0].rearrange("(k p) n -> p k n", p=P)
        w_q = ins["peer_wq"][0].rearrange("(k p) n -> p k n", p=P)

        def piece(kind, j):
            if kind == "embed":
                return [w_in[:, :, 3 * RW:3 * RW + P], w_in[:, :, 3 * RW + P:3 * RW + 2 * P]]
            if kind == "rwkv":
                return [w_in[:, :, x * RW + j * P:x * RW + (j + 1) * P] for x in (0, 1, 2)]
            if kind == "attn":
                return [w_in[:, :, RW_COLS + x * DA + j * P:RW_COLS + x * DA + (j + 1) * P] for x in (0, 1, 2)]
            w = w_out if kind == "out" else w_q
            n = KT if kind == "out" else 2 * PH
            return [w[:, :, i * P:(i + 1) * P] for i in range(3 * j, min(3 * j + 3, n))]

        SETS = []
        for kind, n, j in PHASE_LIST:
            if kind == "project":
                SETS += [("out", i) for i in range(3)] + [("q", i) for i in range(6)]
            else:
                SETS.append((kind, j))
        PER_SEG = 2 * NJ + 1 + 9

        def set_number(kind, s, j):
            base = s.n * PER_SEG
            return base + {"embed": 0, "rwkv": 1 + 2 * j, "attn": 2 + 2 * j, "out": 2 * NJ + 1 + j,
                           "q": 2 * NJ + 4 + j}[kind]

        def weights_in(k):
            return 16 * sum(len(piece(*SETS[i])) for i in range(k % 2, k + 1, 2))

        @block.sync
        def _(sp):
            tl = Tally(sp, None)
            loaded = [0]

            def load_set(k):
                if k < len(SETS):
                    for i, w in enumerate(piece(*SETS[k])):
                        sp.dma_start(wts[:, k % 2, i], w).then_inc(S[f"w{k % 2}"], 16)

            row = x_in[:, 0, 0:P]
            rows = [(MU, "shift_mu", 14), (W0, "rw_w0", 4), (A0, "rw_a0", 4), (KKW, "rw_kk", 4), (KAW, "rw_ka", 4),
                    (RKW, "rw_rk", 4), (LXG, "rw_lnx_g", 4), (LXB, "rw_lnx_b", 4), (SUBG, "da_subln_g", 1)]
            for at, name, n in rows:
                src = ins[name][0]
                if name == "rw_rk":
                    src = src.rearrange("h d -> (h d)")
                sp.dma_start(row[at:at + n, :], src.rearrange("(c p) -> c p", p=P)).then_inc(S["par_in"], 16)
            sp.dma_start(row[SHIFT:SHIFT + 14, :],
                         ins["state_shift"][0, 0, 0].rearrange("(c p) -> c p", p=P)).then_inc(S["par_in"], 16)
            load_set(0)
            sp.dma_start(lora_wa[0:64, :], ins["rw_w2"][0]).then_inc(S["par_in"], 16)
            sp.dma_start(lora_wa[64:128, :], ins["rw_a2"][0]).then_inc(S["par_in"], 16)
            sp.dma_start(lora_g[:, :], ins["rw_g2"][0]).then_inc(S["par_in"], 16)
            for i, name in enumerate(("da_lq1", "da_lk1", "da_lq2", "da_lk2")):
                sp.dma_start(lam_in[:, i, :], ins[name][0].partition_broadcast(P)).then_inc(S["par_in"], 16)
            for i, name in enumerate(("ln2_g", "ln2_b")):
                sp.dma_start(ln2[:, i, :], ins[name][0].partition_broadcast(P)).then_inc(S["par_in"], 16)
            sp.dma_start(rope[:, 0:len(TILES) - 1, :], ins["rope"][0:SEQ].rearrange("(t p) c -> p t c", p=P)).then_inc(S["par_in"], 16)
            sp.dma_start(rope[0:DEC, len(TILES) - 1, :], ins["rope"][SEQ:SEQ + DEC]).then_inc(S["par_in"], 16)
            sp.dma_start(scores[:, 0], ins["peer_subkeys"][0].rearrange("h c n d -> n (h c) d")).then_inc(S["par_in"], 16)
            for e in range(1):
                sp.dma_start(x_in[:, 1, 0:NJ * HD].rearrange("p (j k) -> p j k", j=NJ),
                             ins["state_wkv"][0, 0].rearrange("(j e) v k -> (e v) j k", e=2)).then_inc(S["par_in"], 16)
            sp.wait_ge(S["init_done"], 1)
            sp.sem_inc(S["bar_sp"], 1)

            for kind, s, j in MIX_STEPS:
                out_k, out_v = (k_s, v_s) if s.sample else (k_p, v_p)
                if kind == "embed":
                    enter(sp, "sp", kind, s, j)
                    load_set(set_number("embed", s, 0) + 1)
                    for i, name in enumerate(("ln_in_g", "ln_in_b")):
                        sp.dma_start(ln_mix[:, i, :], ins[name].partition_broadcast(P)).then_inc(S["lnm_in"], 16)
                    for t in range(s.tiles):
                        sp.dma_start(x_in[0:s.rows, t, :], x_rows(s, t)).then_inc(S[f"x_in{t}"], 16)
                    for t in range(s.tiles):
                        tl.next(S["h_ready"])
                        sp.dma_start(h_d[t * P:t * P + s.rows, :], x_in[0:s.rows, t, :]).then_inc(S["h_stored"], 16)
                    tl.next(S["h_stored"], 16 * s.tiles)
                    sp.sem_inc(S["bar_sp"], 1)
                elif kind == "rwkv":
                    enter(sp, "sp", kind, s, j)
                    load_set(set_number("rwkv", s, j) + 1)
                elif kind == "chunks":
                    if s.last:
                        tl.next(S["out_read"])
                        dst = wkv_s if s.sample else wkv_p
                        sp.dma_start(dst[0, 0, 2 * j:2 * j + 2].rearrange("h v k -> (h v) k"), s_out).then_inc(S["st_stored"], 16)
                        tl.next(S["st_stored"], 16)
                    sp.sem_inc(S["bar_sp"], 1)
                elif kind == "attn":
                    enter(sp, "sp", kind, s, j)
                    if s.sample:
                        sp.dma_start(old_k, ins["cache_k"][0, 0, :, j, :].rearrange("(b p) e -> p b e", p=P)).then_inc(S["hist"], 16)
                        sp.dma_start(vals[:, 0:PAST // P], ins["cache_v"][0, 0, :, j, :].rearrange("(b p) e -> p b e", p=P)).then_inc(S["hist"], 16)
                    elif s.past:
                        sp.dma_start(keysT[:, 0:s.past], kt_d[j, :, 0:s.past]).then_inc(S["hist"], 16)
                        sp.dma_start(vals[:, 0:s.past // P], v_p[0, 0, 0:s.past, j, :].rearrange("(b p) e -> p b e", p=P)).then_inc(S["hist"], 16)
                    load_set(set_number("attn", s, j) + 1)
                    for t in range(s.tiles):
                        tl.next(S["roped"])
                        r = slice(s.start + t * P, s.start + t * P + s.rows)
                        sp.dma_start(out_k[0, 0, r, j, :], qk[0:s.rows, t, P:2 * P]).then_inc(S["kv_stored"], 16)
                        sp.dma_start(out_v[0, 0, r, j, :], vals[0:s.rows, s.past // P + t, :]).then_inc(S["kv_stored"], 16)
                    tl.next(S["kv_stored"], 32 * s.tiles)
                    tl.next(S["qkT_read"], 2 * s.tiles)
                    if not s.sample:
                        sp.dma_start(kt_d[j, :, s.past:s.past + s.width], keysT[:, s.past:s.past + s.width]).then_inc(S["kt_stored"], 16)
                        tl.next(S["kt_stored"], 16)
                    sp.sem_inc(S["bar_sp"], 1)
                elif kind == "project":
                    enter(sp, "sp", kind, s, j)
                    for i, name in enumerate(("ln1_g", "ln1_b")):
                        sp.dma_start(ln_mix[:, i, :], ins[name][0].partition_broadcast(P)).then_inc(S["lnm_in"], 16)
                    for t in range(s.tiles):
                        sp.dma_start(x1[0:s.rows, t, :], h_d[t * P:t * P + s.rows, :]).then_inc(S["res_in"], 16)
                    base = set_number("out", s, 0)
                    load_set(base + 1)
                    for i in range(3):
                        tl.next(S["wset"])
                        load_set(base + i + 2)
                    for t in range(s.tiles):
                        tl.next(S["h_ready"])
                        g = s.first_tile + t
                        sp.dma_start(h1_d[g * P:g * P + s.rows, :], x1[0:s.rows, t, :]).then_inc(S["h1_stored"], 16)
                    tl.next(S["h1_stored"], 16 * s.tiles)
                elif kind == "query":
                    base = set_number("q", s, 0)
                    for i in range(6):
                        n = len(piece("q", i))
                        tl.next(S["q_full"], n)
                        if i >= 0 and i < 5:
                            load_set(base + i + 2)
                    sp.sem_inc(S["bar_sp"], 1)
                    if s.last:
                        dst = sh_s if s.sample else sh_p
                        tl.next(S["shift_read"])
                        sp.dma_start(dst[0, 0, 0].rearrange("(c p) -> c p", p=P), shift_rows[:, :]).then_inc(S["shift_stored"], 16)
            sp.wait_ge(S["shift_stored"], 32)

        @block.gpsimd
        def _(pool):
            tl = Tally(pool, S["own_pool"])
            tl.link(pool.memset(ident[:, :], 0.0))
            tl.link(pool.affine_select(out=ident[:, :], in_=ident[:, :], compare_op=ALU.not_equal, fill=1.0, base=0,
                                       pattern=[[-1, P]], channel_multiplier=1))
            tl.link(pool.memset(zeros[:, :], 0.0))
            tl.link(pool.memset(ones2[:, :], 0.0))
            tl.link(pool.memset(mean2[:, :], 0.0))
            for h in halves():
                tl.link(pool.memset(ones2[h, h], 1.0))
                tl.link(pool.memset(mean2[h, h], 1.0 / HD))
            tl.link(pool.memset(causal[:, :, :], 1.0))
            tl.link(pool.memset(lower[:, :, :], 1.0))
            tl.link(pool.memset(first_lo[:, :], 1.0))
            tl.link(pool.memset(restart[:, :], 1.0))
            tl.link(pool.memset(restart[:, 0:SEG:CH], 0.0))
            tl.link(pool.memset(eps_ln[:, :], LN_EPS))
            tl.link(pool.memset(eps_gn[:, :], GN_EPS))
            tl.link(pool.memset(prev[:, :, :], 0.0))
            tl.link(pool.memset(state[:, :, :, :], 0.0))
            tl.link(pool.iota(iota16[:, :], pattern=[[1, TOPK]], base=0, channel_multiplier=0,
                              allow_small_or_imprecise_dtypes=True))

            def keep(out, pattern, base, mult, op=ALU.is_ge):
                tl.link(pool.affine_select(out=out, in_=out, compare_op=op, fill=0.0, base=base, pattern=pattern,
                                           channel_multiplier=mult))
            for h in halves():
                keep(causal[h, 0, :], [[1, CH]], -1, -1)
                keep(causal[h, 1, :], [[1, CH]], 0, -1)
                for l in range(6):
                    w = 1 << l
                    v = lower[h, l, :].rearrange("p (a b c) -> p a b c", b=2, c=w)
                    pat = [[-2 * w, CH // (2 * w)], [0, 2], [0, w]]
                    neg = [[2 * w, CH // (2 * w)], [0, 2], [0, w]]
                    keep(v, pat, 0, 1)
                    keep(v, neg, w - 1, -1)
                    keep(v, [[0, CH // (2 * w)], [1, 2], [0, w]], -1, 0)
                v = first_lo[h, :].rearrange("p (a b) -> p a b", b=2)
                keep(v, [[-2, CH // 2], [-1, 2]], -1, 1, ALU.is_equal)
                keep(v, [[0, CH // 2], [-1, 2]], 0, 0)
            pool.drain().then_inc(S["consts"], 1)

            def gather(what, table, seg, t, i, half, number, used, staged):
                for sem_used in used:
                    pool.wait_ge(sem_used, number + 1)
                    pool.sem_inc(S["parked"], 1)
                mine = stage[0:seg.rows, what, half]
                pool.tensor_copy(mine, idx[0:seg.rows, seg.n % 2, t, bass.ds(i * 2 * PIECE + half * PIECE, PIECE)]).then_inc(staged, 1)
                pool.wait_ge(staged, number + 1)
                pool.sem_inc(S["parked"], 1)
                for n in range(PIECE):
                    slot = v_slot(half, n) if what else u_slot(half, n)
                    pool.indirect_dma_start(
                        out=ring[0:seg.rows, slot, :], out_offset=None, in_=table,
                        in_offset=bass.IndirectOffsetOnAxis(ap=mine[:, n:n + 1].bitcast(U32), axis=0)
                    ).then_inc(s_row[slot], 16)

            def u_piece(g, i, half):
                seg, t = TILES[g]
                gather(0, ins["peer_u"][0], seg, t, i, half, i * 2 + (half + PIECES * g), (S["u_used"],), S["staged_u"])

            def v_piece(g, i, half):
                seg, t = TILES[g]
                gather(1, ins["peer_v"][0], seg, t, i, half, i * 2 + (half + PIECES * g), (S["v_added"], S["v_summed"]), S["staged_v"])

            def units(g, i, half):
                if g < len(TILES):
                    u_piece(g, i, half)
                if g > 0:
                    v_piece(g - 1, i, half)

            def store(g):
                seg, t = TILES[g]
                pool.wait_ge(S["y_ready"], g + 1)
                r = slice(seg.start + t * P, seg.start + t * P + seg.rows)
                pool.dma_start((y_s if seg.sample else y_p)[0, r, :], h1[0:seg.rows, g % 3, :]).then_inc(S["y_stored"], 16)

            for kind, g, arg in order:
                if kind == "open" and g < len(TILES):
                    seg, t = TILES[g]
                    pool.wait_ge(S["idx_ready"], g + 1)
                    if g >= 3:
                        pool.wait_ge(S["y_stored"], 16 * (g - 2))
                    pool.dma_start(h1[0:seg.rows, g % 3, :], h1_d[g * P:g * P + seg.rows, :]).then_inc(S[f"h1_in{g % 3}"], 16)
                elif kind == "u" and arg[1] == 0:
                    u_piece(g, arg[0] // 2, arg[0] % 2)
                elif kind == "v" and arg[1] == 0:
                    v_piece(g, arg[0] // 2, arg[0] % 2)
                    if arg[0] == PIECES // 2 and g >= 1:
                        store(g - 1)
                elif kind == "turns":
                    turns(pool, g, units)
                    store(g - 2)
            store(len(TILES) - 1)
            pool.wait_ge(S["y_stored"], 16 * len(TILES))

        @block.scalar
        def _(act):
            tl = Tally(act, S["own_act"])
            act.wait_ge(S["consts"], 1)
            tl.next(S["par_full"])
            tl.link(act.activation(par[:, :], pm[:, 0, 0:NPAR], ACT.Copy))
            tl.link(act.activation(prev[:, 1, :], par[:, SHIFT:SHIFT + 14], ACT.Copy))
            for i in range(4):
                tl.next(S["sub_full"])
                tl.link(act.activation(skT[:, 4 * i:4 * i + 4, :], pm[:, 1 + i, :].rearrange("p (c n) -> p c n", n=NK), ACT.Copy))
            tl.next(S["sub_full"])
            tl.link(act.activation(state[:, 1, :, :], pm[:, 5, 0:NJ * HD].rearrange("p (j v) -> p j v", j=NJ), ACT.Copy))
            tl.next(S["lam_ready"])
            act.activation(lam_exp[:, :], lam_sum[:, :], ACT.Exp).then_inc(S["lam_exp_ready"], 1)
            act.wait_ge(S["lam_exp_ready"], 1)
            act.wait_ge(S["init_done"], 1)
            act.sem_inc(S["bar_act"], 1)

            def u_part(g, i, half, part):
                pass

            def v_part(g, i, half, part):
                if part == 1:
                    return
                seg, t = TILES[g]
                act.wait_ge(S["v_summed"], i * 2 + (half + 1 + PIECES * g))
                for n in range(on_pe(g)):
                    x = act.activation(diag[0:seg.rows, half, n, 0:seg.rows], ident[0:seg.rows, 0:seg.rows], ACT.Copy,
                                       scale=wgt[0:seg.rows, bass.ds(i * 2 * PIECE + (half * PIECE + n), 1)])
                x.then_inc(S["diag_ready"], 1)

            def units(g, i, half):
                if g > 0:
                    v_part(g - 1, i, half, 0)

            def extra(kind, g):
                if kind == "open" and g > 0:
                    act.wait_ge(S["weight_ready"], g)
                elif kind == "close":
                    if g < len(TILES):
                        rows = TILES[g][0].rows
                        act.wait_ge(S["dot_kept"], PIECES * (g + 1) + 2)
                        act.activation(dots[0:rows, :], dots[0:rows, :], ACT.Gelu).then_inc(S["gelu_done"], 1)
                    if g > 0:
                        rows = TILES[g - 1][0].rows
                        tl.next(S["mv2s"])
                        act.activation(sd2[0:rows, :], mv2[0:rows, 1:2], ACT.Sqrt, bias=eps_ln[0:rows, :]).then_inc(S["sd2s"], 1)

            def mixing():
                for kind, s, j in MIX_STEPS:
                    if kind == "embed":
                        enter(act, "act", kind, s, j)
                        for t in range(s.tiles):
                            tl.next(S["mv"])
                            act.activation(sd1[0:s.rows], mv1[0:s.rows, 1:2], ACT.Sqrt, bias=eps_ln[0:s.rows, :]).then_inc(S["sd"], 1)
                            for i in range(2):
                                tl.next(S["t_full"])
                                act.activation(hT[:, 4 * i:4 * i + 4, sl(s, t)],
                                               pm[:, i, :].rearrange("p (k n) -> p k n", n=P)[:, :, 0:s.rows],
                                               ACT.Copy).then_inc(S["t_read"], 1)
                            yield "tile"
                        for x in range(2):
                            tl.next(S["lora_full"])
                            act.activation(raw2[:, x, 1:1 + s.width], pm[:, 2 + x, 0:s.width], ACT.Copy).then_inc(S["lora_read"], 1)
                        yield "lora"
                        tl.next(S["lora_mixed"])
                        act.activation(wl_al[0:64, 0:s.width], wl_al[0:64, 0:s.width], ACT.Tanh)
                        act.activation(gate_in[:, 0:s.width], gate_in[:, 0:s.width], ACT.Sigmoid)
                        leave(act, "act")
                        yield "end"
                    elif kind == "rwkv":
                        enter(act, "act", kind, s, j)
                        w = s.width
                        for x in (1, 0, 2):
                            tl.next(S["raw_full"])
                            act.activation(raw[:, x, 1:1 + w], pm[:, x, 0:w], ACT.Copy).then_inc(S["raw_read"], 1)
                        tl.next(S["lo_full"])
                        act.activation(lw[:, 0:w], pm[:, 3, 0:w], ACT.Sigmoid, bias=par[:, W0 + j:W0 + j + 1]).then_inc(S["lo_sig"], 1)
                        tl.next(S["lo_full"])
                        act.activation(a_t[:, 0:w], pm[:, 4, 0:w], ACT.Sigmoid, bias=par[:, A0 + j:A0 + j + 1]).then_inc(S["lo_sig"], 1)
                        tl.next(S["lo_full"])
                        act.activation(g_t[:, 0:w], pm[:, 5, 0:w], ACT.Copy).then_inc(S["lo_sig"], 1)
                        yield "raw"
                        yield "shifted"
                        tl.next(S["cum_ready"])
                        act.activation(dec_i[:, 0:w], cum[:, 0:w], ACT.Exp)
                        act.activation(dec_n[:, 0:w], cum[:, 0:w], ACT.Exp, scale=-1.0)
                        act.activation(dec_x[:, 0:w], cumx[:, 0:w], ACT.Exp).then_inc(S["exps"], 1)
                        tl.next(S["n2_full"])
                        act.activation(nrm[:, 0:w], pm[:, 0, 0:w], ACT.Sqrt).then_inc(S["nrm_ready"], 1)
                        yield "decay"
                        tl.next(S["tok_full"])
                        act.activation(tok[:, 0:2, 0:s.chunks, :],
                                       pm[:, 5, :].rearrange("p (x c n) -> p x c n", x=2, c=NCH)[:, :, 0:s.chunks, :],
                                       ACT.Copy).then_inc(S["tok_read"], 1)
                        tl.next(S["tok_full"])
                        act.activation(tok[:, 2, 0:s.chunks, :], pm[:, 0, 0:w].rearrange("p (c n) -> p c n", n=CH),
                                       ACT.Copy).then_inc(S["tok_read"], 1)
                        yield "grams"
                    elif kind == "levels":
                        for l in range(1, 6):
                            tl.next(S["z_full"])
                            act.activation(zs[:, 0:s.chunks, :], pm[:, 1, 0:s.width].rearrange("p (c n) -> p c n", n=CH),
                                           ACT.Copy).then_inc(S["z_read"], 1)
                            yield "level"
                    elif kind == "chunks":
                        w = s.width
                        for c in range(s.chunks):
                            yield "p1"
                            yield "u"
                            if c < s.chunks - 1:
                                yield "state"
                        tl.next(S["y_full"])
                        act.activation(yraw[:, 0:w], pm[:, 5, 0:w], ACT.Copy).then_inc(S["y_read"], 1)
                        yield "state"
                        yield "mean"
                        tl.next(S["var_full"])
                        act.activation(nrm[:, 0:w], pm[:, 4, 0:w], ACT.Sqrt, bias=eps_gn[:, :]).then_inc(S["ysd"], 1)
                        if s.last:
                            tl.next(S["out_full"])
                            act.activation(s_out, pm[:, 0, 0:HD], ACT.Copy).then_inc(S["out_read"], 1)
                        leave(act, "act")
                        yield "variance"
                        yield "end"
                    elif kind == "attn":
                        enter(act, "act", kind, s, j)
                        if s.sample:
                            tl.next(S["old_full"])
                            act.activation(keysT[:, 0:PAST], pm[:, 4, :], ACT.Copy).then_inc(S["old_read"], 1)
                        for t in range(s.tiles):
                            tl.next(S["qkv_full"])
                            act.activation(qk[0:s.rows, t, :], pm[0:s.rows, t, 0:2 * P], ACT.Copy)
                            act.activation(vals[0:s.rows, s.past // P + t, :], pm[0:s.rows, t, 2 * P:3 * P],
                                           ACT.Copy).then_inc(S["qkv_read"], 1)
                        yield "qkv"
                        for t in range(s.tiles):
                            tl.next(S["qkT_full"])
                            act.activation(qT[:, sl(s, t)], pm[:, 2 + t, 0:s.rows], ACT.Copy).then_inc(S["qkT_read"], 1)
                            act.activation(keysT[:, s.past + t * P:s.past + t * P + s.rows], pm[:, 2 + t, P:P + s.rows],
                                           ACT.Copy).then_inc(S["qkT_read"], 1)
                        yield "rope"
                        for t in range(s.tiles):
                            r, nk = s.rows, s.past + t * P + s.rows
                            yield "scores"
                            tl.next(S["max_ready"])
                            for c in range(2):
                                x = act.activation(probs[0:r, c, 0:nk], pm[0:r, 2 * c:2 * c + 2, :].rearrange("p a n -> p (a n)")[:, 0:nk],
                                                   ACT.Exp, bias=negm[0:r, c:c + 1], scale=DA_SCALE, accum_out=zsum[0:r, c:c + 1])
                            x.then_inc(S["prob_ready"], 1)
                            yield "max"
                            nb = (nk + P - 1) // P
                            for b in range((nb + 3) // 4):
                                tl.next(S["attT_full"])
                                n = min(4, nb - 4 * b)
                                full = n if nk >= (4 * b + n) * P else n - 1
                                if full:
                                    x = act.activation(attT[:, 4 * b:4 * b + full, 0:r],
                                                       pm[:, 4 + b, :].rearrange("p (k n) -> p k n", n=P)[:, 0:full, 0:r], ACT.Copy)
                                if full < n:
                                    k = nk % P
                                    x = act.activation(attT[0:k, 4 * b + full, 0:r], pm[0:k, 4 + b, full * P:full * P + r], ACT.Copy)
                                x.then_inc(S["attT_read"], 1)
                            tl.next(S["o_full"])
                            tl.link(act.activation(o_s[0:r], pm[0:r, 0, 0:P], ACT.Copy, scale=rz[0:r, 0:1]))
                            tl.link(act.activation(o_sq[0:r], o_s[0:r], ACT.Square, accum_out=ss[0:r]))
                            act.activation(rms[0:r], ss[0:r], ACT.Sqrt, bias=eps_ln[0:r, :], scale=1.0 / P).then_inc(S["rms_ready"], 1)
                            yield "probs"
                            tl.next(S["oT_full"])
                            act.activation(mixT[:, NJ + j, sl(s, t)], pm[:, 1, 0:r], ACT.Copy, scale=sub_scale[:, :]).then_inc(S["oT_read"], 1)
                            yield "out"
                        leave(act, "act")
                        yield "end"
                    elif kind == "project":
                        enter(act, "act", kind, s, j)
                        for i in range(3):
                            yield "set"
                        for t in range(s.tiles):
                            tl.next(S["mv"])
                            act.activation(sd3[0:s.rows], mv3[0:s.rows, 1:2], ACT.Sqrt, bias=eps_ln[0:s.rows, :]).then_inc(S["sd"], 1)
                            for i in range(2):
                                tl.next(S["t_full"])
                                act.activation(hT[:, 4 * i:4 * i + 4, sl(s, t)],
                                               pm[:, 4 + i, :].rearrange("p (k n) -> p k n", n=P)[:, :, 0:s.rows],
                                               ACT.Copy).then_inc(S["t_read"], 1)
                            yield "tile"
                    elif kind == "query":
                        for c in range(2 * PH):
                            tl.next(S["q_full"])
                            if c >= 2:
                                act.wait_ge(S["qs_full"], s.n * 2 * PH + c - 1)
                            act.activation(qsT[:, c % 2, 0:s.width], pm[:, c % 2, 0:s.width], ACT.Copy).then_inc(S["q_read"], 1)
                            if c % 4 == 3:
                                act.wait_ge(S["qs_full"], s.n * 2 * PH + c + 1)
                                for t in range(s.tiles):
                                    x = act.activation(scores[0:s.rows, t, c - 3:c + 1, :],
                                                       pm[0:s.rows, 2 + t, :].rearrange("p (c n) -> p c n", n=NK), ACT.Copy)
                                x.then_inc(S["qs_read"], 1)
                            yield "query"
                        if s.last:
                            if s.sample:
                                act.wait_ge(S["shift_stored"], 16)
                            tl.next(S["shift_full"])
                            act.activation(shift_rows[:, :], pm[0:14, 4, 0:P], ACT.Copy).then_inc(S["shift_read"], 1)
                    elif kind == "topk":
                        for c in range(2 * PH):
                            yield "keys"
                        for h in range(PH):
                            yield "pairs"
                        tl.next(S["max_exp"])
                        act.activation(t16[0:s.rows], t16[0:s.rows], ACT.Exp).then_inc(S["exp_ready"], 1)
                        yield "ranks"
                        yield "first"
                        yield "second"
                        if j == s.tiles - 1:
                            leave(act, "act")
            interleave(mixing(), u_part, v_part, units, extra, act)

        @block.tensor
        def _(pe):
            tl = Tally(pe, S["own_pe"])
            pe.wait_ge(S["consts"], 1)
            pe.wait_ge(S["par_in"], 16 * 23)
            pe.transpose(pm[:, 0, 0:NPAR], x_in[0:NPAR, 0, 0:P], ident[0:NPAR, 0:NPAR]).then_inc(S["par_full"], 1)
            for i in range(4):
                for c in range(4):
                    x = pe.transpose(pm[:, 1 + i, c * NK:(c + 1) * NK], scores[:, 0, 4 * i + c, :], ident[:, :])
                x.then_inc(S["sub_full"], 1)
            for j in range(NJ):
                for h in halves():
                    x = pe.matmul(pm[h, 5, j * HD:(j + 1) * HD], x_in[h, 1, j * HD:(j + 1) * HD], ident[h, h], start=True, stop=True)
            x.then_inc(S["sub_full"], 1)
            pe.wait_ge(S["init_done"], 1)
            pe.sem_inc(S["bar_pe"], 1)

            def dense(out, lhs, rhs):
                for k in range(KT):
                    x = pe.matmul(out, lhs(k), rhs(k), start=(k == 0), stop=(k == KT - 1))
                return x

            def transpose_tile(s, t, src, bank):
                for i in range(2):
                    if t > 0:
                        tl.next(S["t_read"])
                    for k in range(4):
                        x = pe.transpose(pm[:, bank + i, k * P:k * P + s.rows], src[0:s.rows, t, (4 * i + k) * P:(4 * i + k + 1) * P],
                                         ident[0:s.rows, 0:s.rows])
                    x.then_inc(S["t_full"], 1)

            def per_head(bank, col, width, lhs, rhs, start=True, stop=True):
                for h in halves():
                    x = pe.matmul(pm[h, bank, col:col + width], lhs[h], rhs[h], start=start, stop=stop, skip_group_check=True)
                return x

            def u_part(g, i, half, part):
                pass

            def v_part(g, i, half, part):
                r = slice(0, TILES[g][0].rows)
                in_loop = not isinstance(i, int)
                if part == 0:
                    pe.wait_ge(S["diag_ready"], i * 2 + (half + 1 + PIECES * g))
                for n in range(on_pe(g)):
                    if (n == 0) == (part == 0):
                        slot = v_slot(half, n)
                        pe.wait_ge(s_row[slot], i * 16 + 16 * (ITERS * g + 1))
                        if in_loop:
                            pe.sem_inc(S["parked_pe"], 1)
                        for c in range(2):
                            x = pe.matmul(pacc[r, c, :], diag[r, half, n, r], ring[r, slot, c * 512:(c + 1) * 512],
                                          start=False, stop=False, skip_group_check=True)
                        if n == on_pe(g) - 1:
                            x.then_inc(S["v_summed"], 1)

            def units(g, i, half):
                if g > 0:
                    v_part(g - 1, i, half, 0)
                    v_part(g - 1, i, half, 1)

            def extra(kind, g):
                if g == 0:
                    return
                rows = TILES[g - 1][0].rows
                if kind == "open":
                    if g > 1:
                        pe.wait_ge(S["f_read"], g - 1)
                    pe.wait_ge(S["weight_ready"], g)
                for c in range(2):
                    x = pe.matmul(pacc[0:rows, c, :], zeros[0:rows, 0:rows], h1[0:rows, (g - 1) % 3, c * 512:(c + 1) * 512],
                                  start=(kind == "open"), stop=(kind == "close"), skip_group_check=True)
                if kind == "close":
                    x.then_inc(S["f_ready"], 1)

            def mixing():
                for kind, s, j in MIX_STEPS:
                    if kind == "embed":
                        enter(pe, "pe", kind, s, j)
                        k0 = set_number("embed", s, 0)
                        for t in range(s.tiles):
                            tl.next(S["h_ready"])
                            transpose_tile(s, t, x_in, 0)
                            yield "tile"
                        tl.next(S["t_read"], 2)
                        pe.wait_ge(S[f"w{k0 % 2}"], weights_in(k0))
                        for x in range(2):
                            dense(pm[:, 2 + x, 0:s.width], lambda k: wts[:, k0 % 2, x, k, :], lambda k: hT[:, k, 0:s.width]
                                  ).then_inc(S["lora_full"], 1)
                        leave(pe, "pe")
                        yield "lora"
                        yield "end"
                    elif kind == "rwkv":
                        enter(pe, "pe", kind, s, j)
                        w = s.width
                        k0 = set_number("rwkv", s, j)
                        pe.wait_ge(S[f"w{k0 % 2}"], weights_in(k0))
                        for x in (1, 0, 2):
                            dense(pm[:, x, 0:w], lambda k: wts[:, k0 % 2, x, k, :], lambda k: hT[:, k, 0:w]).then_inc(S["raw_full"], 1)
                        c = slice(j * P, (j + 1) * P)
                        pe.matmul(pm[:, 3, 0:w], lora_wa[0:64, c], wl_al[0:64, 0:w], start=True, stop=True).then_inc(S["lo_full"], 1)
                        pe.matmul(pm[:, 4, 0:w], lora_wa[64:128, c], wl_al[64:128, 0:w], start=True, stop=True).then_inc(S["lo_full"], 1)
                        pe.matmul(pm[:, 5, 0:w], lora_g[:, c], gate_in[:, 0:w], start=True, stop=True).then_inc(S["lo_full"], 1)
                        yield "raw"
                        tl.next(S["sq_ready"])
                        tl.next(S["raw_read"], 3)
                        pe.matmul(pm[:, 0, 0:w], ones2[:, :], sq[:, 0:w], start=True, stop=True).then_inc(S["n2_full"], 1)
                        yield "shifted"
                        yield "decay"
                        tl.next(S["lo_sig"], 3)
                        tl.next(S["kr_ready"])
                        for c in range(s.chunks):
                            x = per_head(1, c * P, P, bt[:, cols(s, c)], kr[:, c].rearrange("p a t -> p (a t)"))
                        x.then_inc(S["g_full"], 1)
                        for c in range(s.chunks):
                            x = per_head(2, c * P, P, kt[:, cols(s, c)], kr[:, c].rearrange("p a t -> p (a t)"))
                        x.then_inc(S["g_full"], 1)
                        for c in range(s.chunks):
                            x = per_head(3, c * CH, CH, kr[:, c, 0, :], bt[:, cols(s, c)])
                        x.then_inc(S["g_full"], 1)
                        pe.matmul(pm[:, 4, 0:w], ones2[:, :], rkk[:, 0:w], start=True, stop=True).then_inc(S["bon_full"], 1)
                        for n, src in enumerate((kt, bt)):
                            for c in range(s.chunks):
                                for h in halves():
                                    x = pe.matmul(pm[h, 5, n * SEG + c * CH:n * SEG + (c + 1) * CH], src[h, cols(s, c)], ident[h, h],
                                                  start=True, stop=True, skip_group_check=True)
                        x.then_inc(S["tok_full"], 1)
                        tl.next(S["nrm_ready"])
                        for c in range(s.chunks):
                            for h in halves():
                                x = pe.matmul(pm[h, 0, cols(s, c)], rkv[h, 2, cols(s, c)], ident[h, h],
                                              start=True, stop=True, skip_group_check=True)
                        x.then_inc(S["tok_full"], 1)
                        yield "grams"
                        tl.next(S["join_ready"])
                    elif kind == "levels":
                        for l in range(1, 6):
                            tl.next(S["x_ready"])
                            for c in range(s.chunks):
                                x = per_head(1, c * CH, CH, joins[:, l - 1, c, :], xm[:, c, :])
                            x.then_inc(S["z_full"], 1)
                            tl.next(S["z_read"])
                            if l < 5:
                                for c in range(s.chunks):
                                    per_head(2, c * CH, CH, xt[:, c, :], zs[:, c, :])
                            for c in range(s.chunks):
                                x = per_head(3, c * CH, CH, zs[:, c, :], xt[:, c, :])
                            x.then_inc(S["xz_full"], 1)
                            yield "level"
                    elif kind == "chunks":
                        st = state[:, 1 if s.sample else 0, j, :]
                        tl.next(S["x_ready"])
                        tl.next(S["tok_read"], 2)
                        for c in range(s.chunks):
                            if c > 0:
                                tl.next(S["st_new"])
                            per_head(0, 0, HD, kr[:, c, 0, :], st, True, False)
                            per_head(0, 0, HD, mk_ak[:, c, 0, :], tok[:, 2, c, :], False, True).then_inc(S["p1_full"], 1)
                            per_head(5, c * CH, CH, st, kr[:, c, 1, :], True, False)
                            per_head(5, c * CH, CH, tok[:, 2, c, :], mk_ak[:, c, 1, :], False, False)
                            yield "p1"
                            tl.next(S["p1_read"])
                            per_head(1, 0, HD, xt[:, c, :], p1s).then_inc(S["u_full"], 1)
                            per_head(2, 0, HD, tok[:, 0, c, :], tok[:, 2, c, :], True, False)
                            yield "u"
                            tl.next(S["u_read"])
                            per_head(2, 0, HD, tok[:, 1, c, :], us, False, True).then_inc(S["s_full"], 1)
                            x = per_head(5, c * CH, CH, us, lt_ab[:, c, 1, :], False, True)
                            if c == s.chunks - 1:
                                x.then_inc(S["y_full"], 1)
                            yield "state"
                        tl.next(S["st_new"])
                        if s.last:
                            for h in halves():
                                x = pe.matmul(pm[h, 0, 0:HD], st[h], ident[h, h], start=True, stop=True)
                            x.then_inc(S["out_full"], 1)
                        w = s.width
                        tl.next(S["y_read"])
                        pe.matmul(pm[:, 3, 0:w], mean2[:, :], yraw[:, 0:w], start=True, stop=True).then_inc(S["mean_full"], 1)
                        yield "mean"
                        tl.next(S["ysq_ready"])
                        pe.matmul(pm[:, 4, 0:w], mean2[:, :], sq[:, 0:w], start=True, stop=True).then_inc(S["var_full"], 1)
                        leave(pe, "pe")
                        yield "variance"
                        yield "end"
                    elif kind == "attn":
                        enter(pe, "pe", kind, s, j)
                        k0 = set_number("attn", s, j)
                        if s.past:
                            tl.next(S["hist"], 32)
                        if s.sample:
                            for b in range(4):
                                x = pe.transpose(pm[:, 4, b * P:(b + 1) * P], old_k[:, b, :], ident[:, :])
                            x.then_inc(S["old_full"], 1)
                        pe.wait_ge(S[f"w{k0 % 2}"], weights_in(k0))
                        for t in range(s.tiles):
                            dense(pm[0:s.rows, t, 0:3 * P].rearrange("p (x n) -> p x n", n=P), lambda k: hT[:, k, sl(s, t)],
                                  lambda k: wts[:, k0 % 2, :, k, :]).then_inc(S["qkv_full"], 1)
                        yield "qkv"
                        for t in range(s.tiles):
                            tl.next(S["roped"])
                            for n in range(2):
                                x = pe.transpose(pm[:, 2 + t, n * P:n * P + s.rows], qk[0:s.rows, t, n * P:(n + 1) * P],
                                                 ident[0:s.rows, 0:s.rows])
                            x.then_inc(S["qkT_full"], 1)
                        yield "rope"
                        tl.next(S["qkT_read"], 2 * s.tiles)
                        if s.sample:
                            tl.next(S["old_read"])
                        for t in range(s.tiles):
                            r, nk = s.rows, s.past + t * P + s.rows
                            if t > 0:
                                tl.next(S["oT_read"])
                            for c in range(2):
                                hc = halves()[c]
                                for n in range(0, nk, 512):
                                    m = min(512, nk - n)
                                    x = pe.matmul(pm[0:r, 2 * c + n // 512, 0:m], qT[hc, sl(s, t)], keysT[hc, n:n + m], start=True, stop=True)
                            x.then_inc(S["sc_full"], 1)
                            yield "scores"
                            yield "max"
                            tl.next(S["att_ready"])
                            nb = (nk + P - 1) // P
                            for b in range(nb):
                                m = min(P, nk - b * P)
                                x = pe.transpose(pm[0:m, 4 + b // 4, (b % 4) * P:(b % 4) * P + r], probs[0:r, 0, b * P:b * P + m], ident[0:r, 0:r])
                                if b % 4 == 3 or b == nb - 1:
                                    x.then_inc(S["attT_full"], 1)
                            tl.next(S["attT_read"], (nb + 3) // 4)
                            for b in range(nb):
                                m = min(P, nk - b * P)
                                x = pe.matmul(pm[0:r, 0, 0:P], attT[0:m, b, 0:r], vals[0:m, b, :], start=(b == 0), stop=(b == nb - 1))
                            x.then_inc(S["o_full"], 1)
                            yield "probs"
                            tl.next(S["o_ready"])
                            pe.transpose(pm[:, 1, 0:r], o_s[0:r], ident[0:r, 0:r]).then_inc(S["oT_full"], 1)
                            yield "out"
                        tl.next(S["oT_read"])
                        leave(pe, "pe")
                        yield "end"
                    elif kind == "project":
                        enter(pe, "pe", kind, s, j)
                        for i in range(3):
                            k0 = set_number("out", s, i)
                            pe.wait_ge(S[f"w{k0 % 2}"], weights_in(k0))
                            for n in range(3 * i, min(3 * i + 3, KT)):
                                for t in range(s.tiles):
                                    x = dense(pm[0:s.rows, 2 * t + n // 4, (n % 4) * P:(n % 4 + 1) * P], lambda k: mixT[:, k, sl(s, t)],
                                              lambda k: wts[:, k0 % 2, n % 3, k, :])
                            x.then_inc(S["wset"], 1)
                            yield "set"
                        for t in range(s.tiles):
                            tl.next(S["h_ready"])
                            transpose_tile(s, t, x1, 4)
                            yield "tile"
                        tl.next(S["t_read"], 2)
                    elif kind == "query":
                        def query(c):
                            k0 = set_number("q", s, c // 3)
                            if c % 3 == 0:
                                pe.wait_ge(S[f"w{k0 % 2}"], weights_in(k0))
                            dense(pm[:, c % 2, 0:s.width], lambda k: wts[:, k0 % 2, c % 3, k, :], lambda k: hT[:, k, 0:s.width]
                                  ).then_inc(S["q_full"], 1)
                        query(0)
                        for c in range(2 * PH):
                            if c + 1 < 2 * PH:
                                query(c + 1)
                            tl.next(S["q_read"])
                            if c % 4 == 0 and c > 0:
                                tl.next(S["qs_read"])
                            for t in range(s.tiles):
                                x = pe.matmul(pm[0:s.rows, 2 + t, (c % 4) * NK:(c % 4 + 1) * NK], qsT[:, c % 2, sl(s, t)], skT[:, c, :],
                                              start=True, stop=True, skip_group_check=True)
                            x.then_inc(S["qs_full"], 1)
                            yield "query"
                        tl.next(S["qs_read"])
                        if s.last:
                            pe.transpose(pm[0:14, 4, 0:P], prev[:, 1 if s.sample else 0, :], ident[:, :]).then_inc(S["shift_full"], 1)
                    elif kind == "topk":
                        for cut in cuts(kind, s):
                            yield cut[0]
                        if j == s.tiles - 1:
                            leave(pe, "pe")
            interleave(mixing(), u_part, v_part, units, extra, pe)

        @block.vector
        def _(v):
            tl = Tally(v, S["own_dve"])
            for free in ("u_used", "v_added", "v_summed", "dot_kept"):
                for half in range(2):
                    v.nop().then_inc(S[free], 1)
            v.wait_ge(S["consts"], 1)
            v.wait_ge(S["par_in"], 16 * 23)
            tl.link(v.tensor_tensor(eye2[:, :], ident[:, 0:HD], ident[:, HD:P], ALU.add))
            for i in range(2):
                x = v.tensor_tensor_reduce(lam_work[:, :], lam_in[:, 2 * i, :], lam_in[:, 2 * i + 1, :], 1.0, 0.0, ALU.mult, ALU.add,
                                           lam_sum[:, i:i + 1])
                if i == 0:
                    tl.link(x)
            tl.told(x, S["lam_ready"])
            v.wait_ge(S["lam_exp_ready"], 1)
            tl.link(v.tensor_tensor(neg_lam[:, :], lam_exp[:, 1:2], lam_exp[:, 0:1], ALU.subtract))
            tl.link(v.tensor_scalar(neg_lam[:, :], neg_lam[:, :], -LAM_INIT, None, ALU.add))
            tl.link(v.tensor_scalar(one_minus_ka[:, :], par[:, KAW:KAW + NJ], -1.0, 1.0, ALU.mult, ALU.add))
            tl.link(v.tensor_scalar(sub_scale[:, :], par[:, SUBG:SUBG + 1], 1.0 - LAM_INIT, None, ALU.mult))
            v.drain().then_inc(S["init_done"], 1)
            v.wait_ge(S["init_done"], 1)
            v.sem_inc(S["bar_dve"], 1)

            def layer_norm(x, stats, mv, sd, r, gain, said, dev, ready):
                for i in range(2):
                    tl.link(v.bn_stats(stats[0:r, i, :], x[:, i * 512:(i + 1) * 512]))
                tl.told(v.bn_aggr(mv[0:r], stats[0:r].rearrange("p a b -> p (a b)")), said)
                tl.next(dev)
                tl.link(v.reciprocal(sd[0:r], sd[0:r]))
                tl.link(v.tensor_scalar(x, x, mv[0:r, 0:1], sd[0:r], ALU.subtract, ALU.mult))
                tl.link(v.tensor_tensor(x, x, gain[0:r, 0, :], ALU.mult))
                tl.told(v.tensor_tensor(x, x, gain[0:r, 1, :], ALU.add), ready)

            def shift(dst, src, w, mu, kept, tmp):
                tl.link(v.tensor_copy(src[:, 0:1], kept))
                tl.link(v.tensor_tensor(tmp[:, 0:w], src[:, 0:w], src[:, 1:w + 1], ALU.subtract))
                tl.link(v.scalar_tensor_tensor(dst, tmp[:, 0:w], mu, src[:, 1:w + 1], ALU.mult, ALU.add))
                tl.link(v.tensor_copy(kept, src[:, w:w + 1]))

            def u_part(g, i, half, part):
                r = slice(0, TILES[g][0].rows)
                if part == 0:
                    v.wait_ge(S["dot_kept"], i * 2 + (half + 1 + PIECES * g))
                for n in range(part * PIECE // 2, (part + 1) * PIECE // 2):
                    slot = u_slot(half, n)
                    v.wait_ge(s_row[slot], i * 16 + 16 * (ITERS * g + 1))
                    x = v.tensor_tensor_reduce(ring[r, slot, :], ring[r, slot, :], h1[r, g % 3, :], 1.0, 0.0, ALU.mult, ALU.add,
                                               dots8[r, half, n:n + 1])
                if part == 1:
                    x.then_inc(S["u_used"], 1)
                    v.wait_ge(S["u_used"], i * 2 + (half + 3 + PIECES * g))
                    v.tensor_copy(dots[r, bass.ds(i * 2 * PIECE + half * PIECE, PIECE)], dots8[r, half, :]).then_inc(S["dot_kept"], 1)

            def v_part(g, i, half, part):
                if part == 0:
                    return
                r = slice(0, TILES[g][0].rows)
                m = PIECE - on_pe(g)
                made = sum(PIECES * (PIECE - on_pe(x)) + 1 for x in range(g)) + half * m + 1
                for n in range(m):
                    slot = v_slot(half, on_pe(g) + n)
                    v.wait_ge(s_row[slot], i * 16 + 16 * (ITERS * g + 1))
                    v.wait_ge(S["acc_made"], i * 2 * m + (made + n))
                    v.scalar_tensor_tensor(acc[r, :], ring[r, slot, :], wgt[r, bass.ds(i * 2 * PIECE + (half * PIECE + on_pe(g) + n), 1)],
                                           acc[r, :], ALU.mult, ALU.add).then_inc(S["acc_made"], 1)
                v.wait_ge(S["acc_made"], i * 2 * m + (made + m))
                v.sem_inc(S["v_added"], 1)

            def units(g, i, half):
                if g < len(TILES):
                    u_part(g, i, half, 0)
                    u_part(g, i, half, 1)
                if g > 0:
                    v_part(g - 1, i, half, 1)

            def extra(kind, g):
                if kind == "open" and g < len(TILES):
                    tl.next(S[f"h1_in{g % 3}"], 16)
                    if g > 0:
                        v.wait_ge(S["weight_ready"], g)
                elif kind == "close":
                    if g > 0:
                        r = slice(0, TILES[g - 1][0].rows)
                        x = h1[r, (g - 1) % 3, :]
                        tl.next(S["f_ready"])
                        tl.link(v.scalar_tensor_tensor(x, x, ALPHA, acc[r, :], ALU.mult, ALU.add))
                        tl.told(v.tensor_tensor(x, x, pacc[r, :, :].rearrange("p a n -> p (a n)"), ALU.add), S["f_read"])
                    if g < len(TILES):
                        seg, t = TILES[g]
                        ru = slice(0, seg.rows)
                        if g > 0:
                            v.wait_ge(S["v_summed"], PIECES * g + 2)
                        tl.next(S["gelu_done"])
                        v.tensor_tensor(wgt[ru, :], dots[ru, :], gates[ru, seg.n % 2, t, :], ALU.mult).then_inc(S["weight_ready"], 1)
                        v.wait_ge(S["weight_ready"], g + 1)
                        v.memset(acc[ru, :], 0.0).then_inc(S["acc_made"], 1)
                    if g > 0:
                        layer_norm(x, st2, mv2, sd2, TILES[g - 1][0].rows, ln2, S["mv2s"], S["sd2s"], S["y_ready"])

            def mixing():
                for kind, s, j in MIX_STEPS:
                    if kind == "embed":
                        enter(v, "dve", kind, s, j)
                        tl.next(S["lnm_in"], 32)
                        for t in range(s.tiles):
                            tl.next(S[f"x_in{t}"], 16)
                            layer_norm(x_in[0:s.rows, t, :], st1, mv1, sd1, s.rows, ln_mix, S["mv"], S["sd"], S["h_ready"])
                            yield "tile"
                        yield "lora"
                        which = 1 if s.sample else 0
                        for x, dst in enumerate((wl_al, gate_in)):
                            tl.next(S["lora_read"])
                            shift(dst[:, 0:s.width], raw2[:, x, :], s.width, par[:, MU + 12 + x:MU + 13 + x], prev[:, which, 12 + x:13 + x], dif)
                        v.drain().then_inc(S["lora_mixed"], 1)
                        leave(v, "dve")
                        yield "end"
                    elif kind == "rwkv":
                        enter(v, "dve", kind, s, j)
                        w = s.width
                        which = 1 if s.sample else 0
                        R, K, V = (rkv[:, x, 0:w] for x in range(3))

                        def chunked(x):
                            return x.rearrange("p (c t) -> p c t", t=CH)
                        yield "raw"
                        for x in (1, 0, 2):
                            tl.next(S["raw_read"])
                            c = 4 * x + j
                            shift(rkv[:, x, 0:w], raw[:, x, :], w, par[:, MU + c:MU + c + 1], prev[:, which, c:c + 1], delta)
                            if x == 1:
                                tl.link(v.tensor_scalar(kk[:, 0:w], K, par[:, KKW + j:KKW + j + 1], None, ALU.mult))
                                tl.told(v.tensor_tensor(sq[:, 0:w], kk[:, 0:w], kk[:, 0:w], ALU.mult), S["sq_ready"])
                        yield "shifted"
                        tl.next(S["lo_sig"])
                        tl.link(v.tensor_scalar(lw[:, 0:w], lw[:, 0:w], DECAY, None, ALU.mult))
                        tl.link(v.tensor_tensor_scan(cum[:, 0:w], restart[:, 0:w], lw[:, 0:w], 0.0, ALU.mult, ALU.add))
                        tl.told(v.tensor_tensor(cumx[:, 0:w], cum[:, 0:w], lw[:, 0:w], ALU.subtract), S["cum_ready"])
                        tl.next(S["lo_sig"], 2)
                        tl.link(v.tensor_scalar(delta[:, 0:w], a_t[:, 0:w], par[:, KAW + j:KAW + j + 1], one_minus_ka[:, j:j + 1], ALU.mult, ALU.add))
                        tl.link(v.tensor_tensor(K, K, delta[:, 0:w], ALU.mult))
                        tl.link(v.scalar_tensor_tensor(rkk[:, 0:w], K, par[:, RKW + j:RKW + j + 1], R, ALU.mult, ALU.mult))
                        yield "decay"
                        tl.next(S["nrm_ready"])
                        tl.link(v.tensor_scalar(nrm[:, 0:w], nrm[:, 0:w], 1e-12, None, ALU.max))
                        tl.link(v.reciprocal(nrm[:, 0:w], nrm[:, 0:w]))
                        tl.link(v.tensor_tensor(kk[:, 0:w], kk[:, 0:w], nrm[:, 0:w], ALU.mult))
                        tl.link(v.scalar_tensor_tensor(sq[:, 0:w], kk[:, 0:w], -1.0, a_t[:, 0:w], ALU.mult, ALU.mult))
                        tl.next(S["exps"])
                        tl.link(v.tensor_tensor(kr[:, 0:s.chunks, 0, :], chunked(kk[:, 0:w]), chunked(dec_x[:, 0:w]), ALU.mult))
                        tl.link(v.tensor_tensor(kr[:, 0:s.chunks, 1, :], chunked(R), chunked(dec_i[:, 0:w]), ALU.mult))
                        tl.link(v.tensor_tensor(kt[:, 0:w], K, dec_n[:, 0:w], ALU.mult))
                        tl.told(v.tensor_tensor(bt[:, 0:w], sq[:, 0:w], dec_n[:, 0:w], ALU.mult), S["kr_ready"])
                        n = s.chunks

                        def gram(bank, width):
                            return pm[:, bank, 0:n * width].rearrange("p (c t) -> p c t", t=width)
                        mask = causal[:, :, :].rearrange("p a t -> p (a t)")[:, None, :].to_broadcast([P, n, P])
                        yield "grams"
                        tl.next(S["g_full"])
                        tl.link(v.tensor_tensor(lt_ab[:, 0:n].rearrange("p c a t -> p c (a t)"), gram(1, P), mask, ALU.mult))
                        tl.next(S["g_full"])
                        tl.link(v.tensor_tensor(mk_ak[:, 0:n].rearrange("p c a t -> p c (a t)"), gram(2, P), mask, ALU.mult))
                        tl.next(S["g_full"])
                        eye = eye2[:, None, :].to_broadcast([P, n, CH])
                        tl.link(v.tensor_tensor(xm[:, 0:n, :], gram(3, CH), first_lo[:, None, :].to_broadcast([P, n, CH]), ALU.mult))
                        tl.link(v.tensor_tensor(xm[:, 0:n, :], xm[:, 0:n, :], eye, ALU.add))
                        tl.link(v.tensor_tensor(xt[:, 0:n, :], lt_ab[:, 0:n, 0, :], lower[:, 0, None, :].to_broadcast([P, n, CH]), ALU.mult))
                        tl.told(v.tensor_tensor(xt[:, 0:n, :], xt[:, 0:n, :], eye, ALU.add), S["x_ready"])
                        tl.told(v.tensor_tensor(joins[:, :, 0:n, :], lt_ab[:, None, 0:n, 0, :].to_broadcast([P, 5, n, CH]),
                                                lower[:, 1:6, None, :].to_broadcast([P, 5, n, CH]), ALU.mult), S["join_ready"])
                        tl.next(S["bon_full"])
                        tl.link(v.tensor_tensor(bonus[:, 0:w], pm[:, 4, 0:w], V, ALU.mult))
                    elif kind == "levels":
                        n = s.chunks
                        for l in range(1, 6):
                            yield "level"
                            tl.next(S["xz_full"])
                            if l < 5:
                                tl.link(v.tensor_tensor(xm[:, 0:n, :], pm[:, 2, 0:s.width].rearrange("p (c t) -> p c t", t=CH), xm[:, 0:n, :], ALU.add))
                            tl.told(v.tensor_tensor(xt[:, 0:n, :], pm[:, 3, 0:s.width].rearrange("p (c t) -> p c t", t=CH), xt[:, 0:n, :], ALU.add),
                                    S["x_ready"])
                    elif kind == "chunks":
                        w = s.width
                        st = state[:, 1 if s.sample else 0, j, :]
                        for c in range(s.chunks):
                            last = dec_i[:, c * CH + CH - 1:c * CH + CH]
                            tl.link(v.tensor_scalar(s_dec, st, last, None, ALU.mult))
                            yield "p1"
                            tl.next(S["p1_full"])
                            tl.told(v.tensor_copy(p1s, pm[:, 0, 0:HD]), S["p1_read"])
                            yield "u"
                            tl.next(S["u_full"])
                            tl.told(v.tensor_copy(us, pm[:, 1, 0:HD]), S["u_read"])
                            yield "state"
                            tl.next(S["s_full"])
                            tl.told(v.scalar_tensor_tensor(st, pm[:, 2, 0:HD], last, s_dec, ALU.mult, ALU.add), S["st_new"])
                        yield "mean"
                        tl.next(S["mean_full"])
                        tl.link(v.tensor_tensor(yraw[:, 0:w], yraw[:, 0:w], pm[:, 3, 0:w], ALU.subtract))
                        tl.told(v.tensor_tensor(sq[:, 0:w], yraw[:, 0:w], yraw[:, 0:w], ALU.mult), S["ysq_ready"])
                        yield "variance"
                        tl.next(S["ysd"])
                        tl.link(v.reciprocal(nrm[:, 0:w], nrm[:, 0:w]))
                        tl.link(v.tensor_tensor(yraw[:, 0:w], yraw[:, 0:w], nrm[:, 0:w], ALU.mult))
                        tl.link(v.tensor_scalar(yraw[:, 0:w], yraw[:, 0:w], par[:, LXG + j:LXG + j + 1], par[:, LXB + j:LXB + j + 1], ALU.mult, ALU.add))
                        tl.link(v.tensor_tensor(yraw[:, 0:w], yraw[:, 0:w], bonus[:, 0:w], ALU.add))
                        tl.link(v.tensor_tensor(mixT[:, j, 0:w], yraw[:, 0:w], g_t[:, 0:w], ALU.mult))
                        leave(v, "dve")
                        yield "end"
                    elif kind == "attn":
                        enter(v, "dve", kind, s, j)
                        yield "qkv"
                        for t in range(s.tiles):
                            tl.next(S["qkv_read"])
                            r = s.rows
                            x = qk[0:r, t, :].rearrange("p (g d) -> p g d", d=HD)
                            xa, xb = x[:, :, 0:8], x[:, :, 8:16]
                            g = s.first_tile + t
                            cos = rope[0:r, g, None, 0:8].to_broadcast([r, 4, 8])
                            sin = rope[0:r, g, None, 8:16].to_broadcast([r, 4, 8])
                            tl.link(v.tensor_tensor(r1[0:r], xa, cos, ALU.mult))
                            tl.link(v.tensor_tensor(r2[0:r], xb, sin, ALU.mult))
                            tl.link(v.tensor_tensor(r3[0:r], xb, cos, ALU.mult))
                            tl.link(v.tensor_tensor(r4[0:r], xa, sin, ALU.mult))
                            tl.link(v.tensor_tensor(xa, r1[0:r], r2[0:r], ALU.subtract))
                            tl.told(v.tensor_tensor(xb, r3[0:r], r4[0:r], ALU.add), S["roped"])
                        yield "rope"
                        for t in range(s.tiles):
                            r, nk = s.rows, s.past + t * P + s.rows
                            yield "scores"
                            tl.next(S["sc_full"])
                            sc2 = pm[0:r, 0:4, :].rearrange("p (c a) n -> p c (a n)", c=2)
                            if not s.sample:
                                tl.link(v.memset(sc2[0:CH, :, nk - CH:nk], -1.0e30))
                            tl.link(v.tensor_reduce(mx[0:r], sc2[:, :, 0:nk], AX.X, ALU.max))
                            tl.told(v.tensor_scalar(negm[0:r], mx[0:r], -DA_SCALE, None, ALU.mult), S["max_ready"])
                            yield "max"
                            tl.next(S["prob_ready"])
                            tl.link(v.reciprocal(rz[0:r], zsum[0:r]))
                            tl.link(v.tensor_scalar(ratio[0:r], zsum[0:r, 0:1], rz[0:r, 1:2], neg_lam[0:r, :], ALU.mult, ALU.mult))
                            tl.told(v.scalar_tensor_tensor(probs[0:r, 0, 0:nk], probs[0:r, 1, 0:nk], ratio[0:r], probs[0:r, 0, 0:nk],
                                                           ALU.mult, ALU.add), S["att_ready"])
                            yield "probs"
                            tl.next(S["rms_ready"])
                            tl.link(v.reciprocal(rms[0:r], rms[0:r]))
                            tl.told(v.tensor_scalar(o_s[0:r], o_s[0:r], rms[0:r], None, ALU.mult), S["o_ready"])
                            yield "out"
                        leave(v, "dve")
                        yield "end"
                    elif kind == "project":
                        enter(v, "dve", kind, s, j)
                        for i in range(3):
                            yield "set"
                        tl.next(S["lnm_in"], 32)
                        tl.next(S["res_in"], 16 * s.tiles)
                        tl.next(S["wset"], 3)
                        for t in range(s.tiles):
                            x = x1[0:s.rows, t, :]
                            tl.link(v.scalar_tensor_tensor(x, x, ALPHA, pm[0:s.rows, 2 * t:2 * t + 2, :].rearrange("p a n -> p (a n)"),
                                                           ALU.mult, ALU.add))
                            layer_norm(x, st3, mv3, sd3, s.rows, ln_mix, S["mv"], S["sd"], S["h_ready"])
                            yield "tile"
                    elif kind == "query":
                        for c in range(2 * PH):
                            yield "query"
                    elif kind == "topk":
                        r, t = s.rows, j
                        if t == 0:
                            tl.next(S["qs_read"], 4)
                            v.wait_ge(S["h1_stored"], 16 * (s.first_tile + s.tiles))
                        for c in range(2 * PH):
                            x = scores[0:r, t, c, :]
                            top16(v, tl, x, work[0:r, :], v16[0:r, c, :], i16[0:r, c, :])
                            yield "keys"
                        tl.link(v.tensor_copy(i16f[0:r], i16[0:r]))
                        one = v16[0:r].rearrange("p (h c) k -> p h c k", c=2)
                        s1, s2 = one[:, :, 0, :], one[:, :, 1, :]
                        left = cand[0:r, :, 0:ROW_A * TOPK].rearrange("p h (a b) -> p h a b", a=ROW_A)
                        rest = cand[0:r, :, ROW_A * TOPK:NCAND].rearrange("p h (a b) -> p h a b", a=ROW_B)
                        tl.link(v.tensor_tensor(left, s1[:, :, 0:ROW_A, None].to_broadcast([r, PH, ROW_A, TOPK]),
                                                s2[:, :, None, :].to_broadcast([r, PH, ROW_A, TOPK]), ALU.add))
                        tl.link(v.tensor_tensor(rest, s1[:, :, ROW_A:TOPK, None].to_broadcast([r, PH, ROW_B, 4]),
                                                s2[:, :, None, 0:4].to_broadcast([r, PH, ROW_B, 4]), ALU.add))
                        for h in range(PH):
                            top16(v, tl, cand[0:r, h, :], work[0:r, 0:NCAND], t16[0:r, h, :], pos[0:r, h, :])
                            yield "pairs"
                        tl.link(v.tensor_copy(hmax[0:r], t16[0:r, :, 0]))
                        tl.told(v.tensor_tensor(t16[0:r], t16[0:r], hmax[0:r, :, None].to_broadcast([r, PH, TOPK]), ALU.subtract), S["max_exp"])
                        p_flat = pos[0:r].rearrange("p h k -> p (h k)")
                        tl.link(v.tensor_scalar(posb[0:r, 0], p_flat, 4, None, ALU.logical_shift_right))
                        tl.link(v.tensor_scalar(posb[0:r, 1], p_flat, 15, None, ALU.bitwise_and))
                        tl.link(v.tensor_scalar(posb[0:r, 2], p_flat, 2, None, ALU.logical_shift_right))
                        tl.link(v.tensor_scalar(posb[0:r, 3], p_flat, 3, None, ALU.bitwise_and))

                        def flat(x):
                            return x[0:r].rearrange("p h k -> p (h k)")
                        tl.link(v.tensor_scalar(flat(pos_f), p_flat, float(ROW_A * TOPK), None, ALU.is_ge))
                        for out, lo, hi, off in ((af, 0, 2, -12.0), (bf, 1, 3, 0.0)):
                            tl.link(v.tensor_copy(flat(out), posb[0:r, lo]))
                            tl.link(v.scalar_tensor_tensor(flat(e1), posb[0:r, hi], off, flat(out), ALU.add, ALU.subtract))
                            tl.link(v.tensor_tensor(flat(e1), flat(e1), flat(pos_f), ALU.mult))
                            tl.link(v.tensor_tensor(flat(out), flat(out), flat(e1), ALU.add))
                        yield "ranks"
                        keys = i16f[0:r].rearrange("p (h c) k -> p h c k", c=2)
                        for c, (rank, out) in enumerate(((af, e1), (bf, e2))):
                            tl.link(v.tensor_tensor(hot[0:r], flat(rank)[:, :, None].to_broadcast([r, SLOTS, TOPK]),
                                                    iota16[0:r, None, :].to_broadcast([r, SLOTS, TOPK]), ALU.is_equal))
                            hot4 = hot[0:r].rearrange("p (h e) k -> p h e k", h=PH)
                            tl.link(v.tensor_tensor(hot4, hot4, keys[:, :, c, None, :].to_broadcast([r, PH, TOPK, TOPK]), ALU.mult))
                            tl.link(v.tensor_reduce(flat(out), hot[0:r], AX.X, ALU.add))
                            if c == 0:
                                yield "first"
                        tl.link(v.scalar_tensor_tensor(idx[0:r, s.n % 2, t, :], flat(e1), float(NK), flat(e2), ALU.mult, ALU.add))
                        tl.next(S["exp_ready"])
                        tl.link(v.tensor_reduce(hmax[0:r], t16[0:r], AX.X, ALU.add))
                        tl.link(v.reciprocal(hmax[0:r], hmax[0:r]))
                        tl.told(v.tensor_tensor(gates[0:r, s.n % 2, t, :].rearrange("p (h k) -> p h k", h=PH), t16[0:r],
                                                hmax[0:r, :, None].to_broadcast([r, PH, TOPK]), ALU.mult), S["idx_ready"])
                        if t == s.tiles - 1:
                            leave(v, "dve")
                        yield "second"
            interleave(mixing(), u_part, v_part, units, extra, v)


def top16(v, tl, x, work, values, places):
    tl.link(v.max(values[:, 0:8], x))
    tl.link(v.max_index(places[:, 0:8], values[:, 0:8], x))
    tl.link(v.match_replace(work, values[:, 0:8], x, LOW))
    tl.link(v.max(values[:, 8:16], work))
    tl.link(v.max_index(places[:, 8:16], values[:, 8:16], work))


_INS = ['x_prompt', 'x_sample', 'cache_k', 'cache_v', 'state_wkv', 'state_shift', 'ln_in_g', 'ln_in_b',
        'w_in', 'shift_mu', 'rw_w0', 'rw_w2', 'rw_a0', 'rw_a2', 'rw_g2', 'rw_kk', 'rw_ka', 'rw_rk', 'rw_lnx_g',
        'rw_lnx_b', 'da_lq1', 'da_lk1', 'da_lq2', 'da_lk2', 'da_subln_g', 'w_out', 'ln1_g', 'ln1_b',
        'peer_wq', 'peer_subkeys', 'peer_u', 'peer_v', 'ln2_g', 'ln2_b']
_OUTS = [(1, 1024, 1024), (1, 64, 1024), (1, 1, 1024, 4, 128), (1, 1, 1024, 4, 128), (1, 1, 8, 64, 64),
         (1, 1, 1, 1792), (1, 1, 64, 4, 128), (1, 1, 64, 4, 128), (1, 1, 8, 64, 64), (1, 1, 1, 1792)]


def rope_tables():
    half = ROT // 2
    pos = np.concatenate([np.arange(SEQ), PAST + np.arange(DEC)]).astype(np.float32)
    inv = np.power(np.float32(THETA), -np.arange(half, dtype=np.float32) * np.float32(2.0 / ROT)).astype(np.float32)
    ang = pos[:, None] * inv[None, :]
    return np.concatenate([np.cos(ang), np.sin(ang)], 1).astype(np.float32)


def kernel(**inputs):
    import concourse.bacc as bacc
    from concourse.bass_utils import run_bass_kernel_spmd as run

    nc = bacc.Bacc("TRN2", target_bir_lowering=False, num_devices=1)
    arrays, ins = {}, {}
    for name in _INS:
        arrays[f"in_{name}"] = np.ascontiguousarray(inputs[name])
        ins[name] = nc.dram_tensor(f"in_{name}", arrays[f"in_{name}"].shape, F32, kind="ExternalInput").ap()
    arrays["in_rope"] = rope_tables()
    ins["rope"] = nc.dram_tensor("in_rope", arrays["in_rope"].shape, F32, kind="ExternalInput").ap()
    outs = [nc.dram_tensor(f"out_{i}", shape, F32, kind="ExternalOutput").ap() for i, shape in enumerate(_OUTS)]
    build(nc, ins, outs)
    r = run(nc, [arrays], core_ids=[0])
    return tuple(r.results[0][f"out_{i}"] for i in range(len(_OUTS)))
```
